# Optimizing a Trainium2 kernel written in Bass

```python
import jax, jax.numpy as jnp
from jax import lax
import numpy as np

D_MODEL = 2048
BATCH = 1
SEQ = 512
DEPTH = 1
DEC_BATCH = 8
DEC_SEQ = 4
PAST_LEN = 2048
PAGE_SIZE = 128

POOL_DIM = D_MODEL // 2
POOL_WINDOWS = (2, 4, 8, 16)
N_POOL_GROUPS = len(POOL_WINDOWS)
POOL_GROUP = POOL_DIM // N_POOL_GROUPS
POOL_HIST = max(POOL_WINDOWS) - 1
ATTN_DIM = D_MODEL - POOL_DIM
HEAD_DIM = 128
N_HEADS = ATTN_DIM // HEAD_DIM
ROT_DIM = HEAD_DIM // 4
ROPE_THETA = 500000.0
MOBA_BLOCK = 256
MOBA_TOPK = 3
Q_CHUNK = 32
D_FF = 5632
CONV_W = 3
EPS = 1e-6

kernel_name = 'hymba_pool_moba_convffn_step'

def rmsnorm(x, g):
    xf = x.astype(jnp.float32)
    y = xf * lax.rsqrt(jnp.mean(xf * xf, axis=-1, keepdims=True) + EPS)
    return (y * g.astype(jnp.float32)).astype(x.dtype)

def rope(x, pos):
    half = ROT_DIM // 2
    inv = ROPE_THETA ** (-jnp.arange(half, dtype=jnp.float32) * (2.0 / ROT_DIM))
    ang = pos.astype(jnp.float32)[:, None] * inv[None, :]
    cos = jnp.cos(ang)[:, None, :]
    sin = jnp.sin(ang)[:, None, :]
    xr = x[..., :ROT_DIM].astype(jnp.float32)
    x1, x2 = xr[..., :half], xr[..., half:]
    rot = jnp.concatenate([x1 * cos - x2 * sin, x2 * cos + x1 * sin], axis=-1)
    return jnp.concatenate([rot.astype(x.dtype), x[..., ROT_DIM:]], axis=-1)

def pool_mix(u, hist, start, w_pool, pool_scale):
    B, L, _ = u.shape
    ext = jnp.concatenate([hist.astype(u.dtype), u], axis=1).astype(jnp.float32)
    cs = jnp.concatenate([jnp.zeros((B, 1, POOL_DIM), jnp.float32),
                          jnp.cumsum(ext, axis=1)], axis=1)
    pos = start + jnp.arange(L)
    end = cs[:, POOL_HIST + 1:]
    means = []
    for g, w in enumerate(POOL_WINDOWS):
        sl = slice(g * POOL_GROUP, (g + 1) * POOL_GROUP)
        begin = cs[:, POOL_HIST + 1 - w: POOL_HIST + 1 - w + L, sl]
        cnt = jnp.minimum(pos + 1, w).astype(jnp.float32)[None, :, None]
        means.append((end[..., sl] - begin) / cnt)
    d = (jnp.concatenate(means, axis=-1) - u.astype(jnp.float32)).astype(u.dtype)
    d = d.reshape(B, L, N_POOL_GROUPS, POOL_GROUP)
    y = jnp.einsum('blgc,gcd->blgd', d, w_pool).reshape(B, L, POOL_DIM)
    return y * pool_scale

def moba_prompt(q, k, v):
    B, H, S, D = q.shape
    nb = -(-S // MOBA_BLOCK)
    pad = nb * MOBA_BLOCK - S
    kp = jnp.pad(k, ((0, 0), (0, 0), (0, pad), (0, 0)))
    vp = jnp.pad(v, ((0, 0), (0, 0), (0, pad), (0, 0)))
    kb = kp.reshape(B, H, nb, MOBA_BLOCK, D)
    vb = vp.reshape(B, H, nb, MOBA_BLOCK, D)
    kmean = jnp.mean(kb.astype(jnp.float32), axis=3)
    n_sel = min(MOBA_TOPK, nb - 1)
    n_s = n_sel * MOBA_BLOCK
    scale = HEAD_DIM ** -0.5
    bidx = jnp.arange(B)[:, None, None, None]
    hidx = jnp.arange(H)[None, :, None, None]

    def chunk(c):
        q0 = c * Q_CHUNK
        qc = lax.dynamic_slice_in_dim(q, q0, Q_CHUNK, axis=2)
        qpos = q0 + jnp.arange(Q_CHUNK)
        blk = q0 // MOBA_BLOCK
        own_k = lax.dynamic_slice_in_dim(kp, blk * MOBA_BLOCK, MOBA_BLOCK, axis=2)
        own_v = lax.dynamic_slice_in_dim(vp, blk * MOBA_BLOCK, MOBA_BLOCK, axis=2)
        kpos = blk * MOBA_BLOCK + jnp.arange(MOBA_BLOCK)
        s_own = jnp.einsum('bhqd,bhkd->bhqk', qc, own_k).astype(jnp.float32) * scale
        s_own = jnp.where(kpos[None, :] <= qpos[:, None], s_own, -jnp.inf)
        if n_sel == 0:
            p = jax.nn.softmax(s_own, axis=-1).astype(v.dtype)
            return jnp.einsum('bhqk,bhkd->bhqd', p, own_v)
        gate = jnp.einsum('bhqd,bhnd->bhqn', qc.astype(jnp.float32), kmean)
        gate = jnp.where(jnp.arange(nb) < blk, gate, -jnp.inf)
        _, sel = lax.top_k(gate, n_sel)
        ok = sel < blk
        ks = kb[bidx, hidx, sel]
        vs = vb[bidx, hidx, sel]
        s_sel = jnp.einsum('bhqd,bhqnkd->bhqnk', qc, ks).astype(jnp.float32) * scale
        s_sel = jnp.where(ok[..., None], s_sel, -jnp.inf).reshape(B, H, Q_CHUNK, n_s)
        p = jax.nn.softmax(jnp.concatenate([s_sel, s_own], axis=-1), axis=-1)
        p_sel = p[..., :n_s].reshape(B, H, Q_CHUNK, n_sel, MOBA_BLOCK).astype(v.dtype)
        out = jnp.einsum('bhqnk,bhqnkd->bhqd', p_sel, vs)
        return out + jnp.einsum('bhqk,bhkd->bhqd', p[..., n_s:].astype(v.dtype), own_v)

    outs = lax.map(chunk, jnp.arange(S // Q_CHUNK))
    return outs.transpose(1, 2, 0, 3, 4).reshape(B, H, S, D)

def moba_sample(q, k_new, v_new, cache_k, cache_v, page_table):
    Bd, H, L, D = q.shape
    n_pages = page_table.shape[1]
    ppb = MOBA_BLOCK // PAGE_SIZE
    nb_past = (n_pages * PAGE_SIZE) // MOBA_BLOCK
    n_tail = n_pages - nb_past * ppb
    n_sel = min(MOBA_TOPK, nb_past)
    scale = HEAD_DIM ** -0.5
    s_parts, v_parts = [], []
    if n_sel > 0:
        blk_pages = page_table[:, :nb_past * ppb].reshape(Bd, nb_past, ppb)
        page_sums = jnp.sum(cache_k.astype(jnp.float32), axis=2)
        kmean = jnp.sum(page_sums[blk_pages], axis=2) / MOBA_BLOCK
        gate = jnp.einsum('bhqd,bnhd->bhqn', q.astype(jnp.float32), kmean)
        _, sel = lax.top_k(gate, n_sel)
        phys = blk_pages[jnp.arange(Bd)[:, None, None, None], sel]
        hidx = jnp.arange(H)[None, :, None, None, None]
        k_sel = cache_k[phys, hidx].reshape(Bd, H, L, n_sel * MOBA_BLOCK, D)
        v_sel = cache_v[phys, hidx].reshape(Bd, H, L, n_sel * MOBA_BLOCK, D)
        s_parts.append(jnp.einsum('bhqd,bhqkd->bhqk', q, k_sel).astype(jnp.float32) * scale)
        v_parts.append((v_sel, True))
    if n_tail > 0:
        tail_phys = page_table[:, nb_past * ppb:]
        k_t = cache_k[tail_phys].transpose(0, 2, 1, 3, 4).reshape(Bd, H, n_tail * PAGE_SIZE, D)
        v_t = cache_v[tail_phys].transpose(0, 2, 1, 3, 4).reshape(Bd, H, n_tail * PAGE_SIZE, D)
        s_parts.append(jnp.einsum('bhqd,bhkd->bhqk', q, k_t).astype(jnp.float32) * scale)
        v_parts.append((v_t, False))
    causal = jnp.tril(jnp.ones((L, L), dtype=bool))
    s_new = jnp.einsum('bhqd,bhkd->bhqk', q, k_new).astype(jnp.float32) * scale
    s_parts.append(jnp.where(causal, s_new, -jnp.inf))
    v_parts.append((v_new, False))
    p = jax.nn.softmax(jnp.concatenate(s_parts, axis=-1), axis=-1)
    out = None
    off = 0
    for sc, (vals, per_query) in zip(s_parts, v_parts):
        n = sc.shape[-1]
        pp = p[..., off:off + n].astype(vals.dtype)
        off += n
        term = (jnp.einsum('bhqk,bhqkd->bhqd', pp, vals) if per_query
                else jnp.einsum('bhqk,bhkd->bhqd', pp, vals))
        out = term if out is None else out + term
    return out

def conv_ffn(h, conv_hist, w_gate, w_up, conv_w, conv_b, w_down):
    L = h.shape[1]
    gt = h @ w_gate
    ext = jnp.concatenate([conv_hist.astype(gt.dtype), gt], axis=1)
    c = conv_b
    for j in range(CONV_W):
        c = c + ext[:, j:j + L] * conv_w[j]
    f = jax.nn.gelu(c, approximate=True) * (h @ w_up)
    return f @ w_down, ext[:, L:]

def decoder_layer(x, pool_hist, conv_hist, start, attend, lp):
    B, L, _ = x.shape
    h = rmsnorm(x, lp['g_mix_pre'])
    proj = h @ lp['w_in']
    u = proj[..., :POOL_DIM]
    qkv = proj[..., POOL_DIM:].reshape(B, L, 3, N_HEADS, HEAD_DIM)
    pos = start + jnp.arange(L)
    q = rope(qkv[:, :, 0], pos).transpose(0, 2, 1, 3)
    k = rope(qkv[:, :, 1], pos).transpose(0, 2, 1, 3)
    v = qkv[:, :, 2].transpose(0, 2, 1, 3)
    pooled = pool_mix(u, pool_hist, start, lp['w_pool'], lp['pool_scale'])
    attn = attend(q, k, v).transpose(0, 2, 1, 3).reshape(B, L, ATTN_DIM)
    mix = jnp.concatenate([pooled.astype(x.dtype), attn.astype(x.dtype)], axis=-1) @ lp['w_out']
    x = x + rmsnorm(mix, lp['g_mix_post'])
    f, new_conv = conv_ffn(rmsnorm(x, lp['g_ffn_pre']), conv_hist, lp['w_gate'], lp['w_up'],
                           lp['conv_w'], lp['conv_b'], lp['w_down'])
    x = x + rmsnorm(f, lp['g_ffn_post'])
    new_pool = jnp.concatenate([pool_hist.astype(u.dtype), u], axis=1)[:, L:]
    return x, k, v, new_pool, new_conv

def setup_inputs(seed: int = 0) -> dict:
    key = jax.random.key(seed)
    ks = jax.random.split(key, 24)
    n_pages = PAST_LEN // PAGE_SIZE
    n_used = DEC_BATCH * n_pages
    n_phys = n_used + n_used // 4

    def nrm(k, shape, s=1.0):
        return s * jax.random.normal(k, shape, jnp.float32)

    perm = jax.random.permutation(ks[0], n_phys)
    page_table = perm[:n_used].reshape(DEC_BATCH, n_pages).astype(jnp.int32)
    mix_w = POOL_DIM + ATTN_DIM
    return {
        'x_prompt': nrm(ks[1], (BATCH, SEQ, D_MODEL)),
        'x_sample': nrm(ks[2], (DEC_BATCH, DEC_SEQ, D_MODEL)),
        'cache_k': nrm(ks[3], (DEPTH, n_phys, N_HEADS, PAGE_SIZE, HEAD_DIM)),
        'cache_v': nrm(ks[4], (DEPTH, n_phys, N_HEADS, PAGE_SIZE, HEAD_DIM)),
        'state_pool': nrm(ks[5], (DEPTH, DEC_BATCH, POOL_HIST, POOL_DIM)),
        'state_conv': nrm(ks[6], (DEPTH, DEC_BATCH, CONV_W - 1, D_FF)),
        'page_table': page_table,
        'w_in': nrm(ks[7], (DEPTH, D_MODEL, POOL_DIM + 3 * ATTN_DIM), D_MODEL ** -0.5),
        'w_pool': nrm(ks[8], (DEPTH, N_POOL_GROUPS, POOL_GROUP, POOL_GROUP), POOL_GROUP ** -0.5),
        'pool_scale': 1.0 + nrm(ks[9], (DEPTH, POOL_DIM), 0.1),
        'w_out': nrm(ks[10], (DEPTH, mix_w, D_MODEL), mix_w ** -0.5),
        'g_mix_pre': 1.0 + nrm(ks[11], (DEPTH, D_MODEL), 0.05),
        'g_mix_post': 1.0 + nrm(ks[12], (DEPTH, D_MODEL), 0.05),
        'w_gate': nrm(ks[13], (DEPTH, D_MODEL, D_FF), D_MODEL ** -0.5),
        'w_up': nrm(ks[14], (DEPTH, D_MODEL, D_FF), D_MODEL ** -0.5),
        'conv_w': nrm(ks[15], (DEPTH, CONV_W, D_FF), CONV_W ** -0.5),
        'conv_b': nrm(ks[16], (DEPTH, D_FF), 0.02),
        'w_down': nrm(ks[17], (DEPTH, D_FF, D_MODEL), D_FF ** -0.5),
        'g_ffn_pre': 1.0 + nrm(ks[18], (DEPTH, D_MODEL), 0.05),
        'g_ffn_post': 1.0 + nrm(ks[19], (DEPTH, D_MODEL), 0.05),
    }

def reference(x_prompt, x_sample, cache_k, cache_v, state_pool, state_conv, page_table,
              w_in, w_pool, pool_scale, w_out, g_mix_pre, g_mix_post,
              w_gate, w_up, conv_w, conv_b, w_down, g_ffn_pre, g_ffn_post):
    past_len = page_table.shape[1] * PAGE_SIZE
    B = x_prompt.shape[0]
    yp, ys = x_prompt, x_sample
    kp_l, vp_l, ks_l, vs_l, pp_l, ps_l, cp_l, cs_l = [], [], [], [], [], [], [], []
    for l in range(DEPTH):
        lp = {'w_in': w_in[l], 'w_pool': w_pool[l], 'pool_scale': pool_scale[l],
              'w_out': w_out[l], 'g_mix_pre': g_mix_pre[l], 'g_mix_post': g_mix_post[l],
              'w_gate': w_gate[l], 'w_up': w_up[l], 'conv_w': conv_w[l], 'conv_b': conv_b[l],
              'w_down': w_down[l], 'g_ffn_pre': g_ffn_pre[l], 'g_ffn_post': g_ffn_post[l]}
        zero_pool = jnp.zeros((B, POOL_HIST, POOL_DIM), x_prompt.dtype)
        zero_conv = jnp.zeros((B, CONV_W - 1, D_FF), x_prompt.dtype)
        yp, kp, vp, pp, cp = decoder_layer(yp, zero_pool, zero_conv, 0, moba_prompt, lp)
        ck, cv = cache_k[l], cache_v[l]
        attend_s = lambda q, k, v: moba_sample(q, k, v, ck, cv, page_table)
        ys, ksn, vsn, ps, cs = decoder_layer(ys, state_pool[l], state_conv[l], past_len, attend_s, lp)
        kp_l.append(kp); vp_l.append(vp); ks_l.append(ksn); vs_l.append(vsn)
        pp_l.append(pp); ps_l.append(ps); cp_l.append(cp); cs_l.append(cs)
    return (yp, ys, jnp.stack(kp_l), jnp.stack(vp_l), jnp.stack(ks_l), jnp.stack(vs_l),
            jnp.stack(pp_l), jnp.stack(ps_l), jnp.stack(cp_l), jnp.stack(cs_l))


_drawn_inputs = setup_inputs


def setup_inputs(seed=0):
    import zlib

    import numpy as np

    out = dict(_drawn_inputs(seed))
    spreads = {}
    factors = {'conv_b': 4.924}
    for name, (base, spread) in spreads.items():
        noise = np.random.default_rng([zlib.crc32(name.encode()), seed]).standard_normal(out[name].shape)
        drawn = base * np.exp(spread * noise) if base else spread * noise
        out[name] = __import__('jax').numpy.asarray(drawn.astype(out[name].dtype))
    for name, factor in factors.items():
        out[name] = (out[name] * factor).astype(out[name].dtype)
    return out
```

```python
from contextlib import ExitStack

import concourse.bass as bass
from concourse import mybir

F32 = mybir.dt.float32
F32R = mybir.dt.float32r
I32 = mybir.dt.int32
ALU = mybir.AluOpType
ACT = mybir.ActivationFunctionType
AX = mybir.AxisListType

P = 128
D = 2048
KT = D // P
SEQ = 512
DB, DL = 8, 4
NS = DB * DL
NT = SEQ + NS
HN = NT // 2
NH = 8
PAGES = 16
PAGE = 128
N_PHYS = 160
NBLK = PAGES // 2
TOPK = 3
HC = NH * DL
FF = 5632
FT = FF // P
CH = 4
NCH = FT // CH
HIST = 15
SEG = HIST + DL
EXT = HIST + SEQ + DB * SEG
WINDOWS = (16, 8, 4, 2)
CSEG = 2 + DL
CEXT = 2 + SEQ + DB * CSEG
TAIL = 2 + 2 * DB
NPAR = 4 + 2 * DB
SCALE = float(P) ** -0.5
NEG = -1.0e30
EPS = 1.0e-6
RING = 4
LEAD = 3
G_POOL = 16
G_OUT = G_POOL + 4
G_FF = G_OUT + 8
G_CH = CH + 8
Q_POOL = 32
Q_OUT = Q_POOL + 1
Q_FF = Q_OUT + 16
Q_CH = 2 * CH + 4
UNITS = 4 * (Q_FF + NCH * Q_CH)


def build(nc, xT, units, kcache, vcache, table, gains, pool_hist, conv_par, rope_tab, consts,
          yT, kT_out, vT_out, ext_out, tail_out):
    with ExitStack() as ctx:
        def sb(name, shape, dt=F32):
            return ctx.enter_context(nc.sbuf_tensor(name, shape, dt))

        def sem(name):
            return ctx.enter_context(nc.semaphore(name))

        act_hi = sb("act_hi", [P, KT, NT], F32R)
        act_lo = sb("act_lo", [P, KT, NT], F32R)
        w_raw = sb("w_raw", [P, RING, 2, 256])
        w_hi = sb("w_hi", [P, RING, 2, 256], F32R)
        w_lo = sb("w_lo", [P, RING, 2, 256], F32R)
        R1 = NH * NT + NH * EXT
        reg1 = sb("region1", [P, R1])
        x_in = reg1[:, 0:KT * NT].rearrange("p (k n) -> p k n", k=KT)
        qT = reg1[:, 0:NH * NT].rearrange("p (h n) -> p h n", h=NH)
        kT = reg1[:, NH * NT:2 * NH * NT].rearrange("p (h n) -> p h n", h=NH)
        ext = reg1[:, NH * NT:R1].rearrange("p (t n) -> p t n", t=NH)
        prob = reg1[:, 2 * NH * NT:2 * NH * NT + 1024].rearrange("p (s n) -> p s n", s=2)
        acc = reg1[:, 0:KT * NT].rearrange("p (k n) -> p k n", k=KT)
        par = reg1[:, KT * NT:KT * NT + FT * NPAR].rearrange("p (t n) -> p t n", t=FT)
        R2 = 3 * 4096 + NH * P
        base2 = nc.sbuf_base
        reg2 = sb("region2", [P, R2])
        assert nc.sbuf_base - base2 == 4 * R2
        v_tok = reg2[:, 0:4096].rearrange("p (h t d) -> p h t d", h=NH, t=4)
        s_all = reg2[:, 4096:8192].rearrange("p (b n) -> p b n", b=DB)
        pages = reg2[:, 8192:12288].rearrange("p (s n) -> p s n", s=RING)
        v_new = reg2[0:HC, 12288:R2].rearrange("p (b d) -> p b d", b=DB)
        o_all = reg2[:, 0:8192].rearrange("p (a n) -> p a n", a=2)[:, :, 0:NH * P]
        hist_in = reg2[:, 0:NH * DB * HIST]
        win = reg2[:, 1024:1024 + 4 * EXT].rearrange("p (s t n) -> p s t n", s=2, t=2)
        x2 = reg2[:, 0:KT * NT].rearrange("p (k n) -> p k n", k=KT)
        f_hi = nc.alloc_sbuf_tensor_at("f_hi", [P, CH, NT], F32R, offset=base2 + 4 * KT * NT)
        f_lo = nc.alloc_sbuf_tensor_at("f_lo", [P, CH, NT], F32R, offset=base2 + 4 * (KT + CH) * NT)
        assert (KT + 2 * CH) * NT <= R2 and FT * NPAR <= R1 - KT * NT
        scratch = sb("scratch", [P, 4, CEXT])
        stage = scratch[:, 0:2, 0:NT]
        sq = scratch[:, 0:2, 0:NT]
        probT = scratch[:, :, :].rearrange("p a n -> p (a n)")[:, 0:4 * SEQ].rearrange("p (k n) -> p k n", k=4)
        swap = scratch[0:32, 2, 0:NT]
        sq_sum = scratch[:, 3, 0:NT]
        tmp = scratch[:, 2, 0:NT]
        g_ext, conv, f_buf = scratch[:, 0, :], scratch[:, 1, :], scratch[:, 2, 0:NT]
        rstd = sb("rstd", [P, NT])
        shared = sb("shared", [P, 2, NT])
        cos_t, sin_t = shared[0:32, 0, :], shared[0:32, 1, :]
        p_seq = shared[:, :, 0:PAGES * HC]
        tails = shared[:, :, :].rearrange("p a n -> p (a n)")[:, 0:FT * TAIL].rearrange("p (t n) -> p t n", t=FT)
        cst = sb("cst", [P, 128 + 128 + 128 + 32 + 64 + 64])
        ident, ones, causal = cst[:, 0:128], cst[:, 128:256], cst[:, 256:384]
        new_mask = cst[0:NS, 384:416]
        below = cst[0:NS, 416:480].rearrange("p (i j) -> p i j", i=NBLK)
        corr = cst[:, 480:544].rearrange("p (w n) -> p w n", w=4)
        gain = sb("gain", [P, 4 * KT + NH])
        g_pre, g_post, g_fpre, g_fpost = (gain[:, i * KT:(i + 1) * KT] for i in range(4))
        pscale = gain[:, 4 * KT:]
        q_blk = sb("q_blk", [P, NH * (HC + DL)])
        p_new = sb("p_new", [HC, DB, HC])
        q_dec = sb("q_dec", [P, DB, HC])
        p_newT = q_dec[0:HC]
        v_dec = sb("v_dec", [P, DB, HC])
        gate = sb("gate", [HC, DB, NBLK])
        bmax = sb("bmax", [HC, DB, NBLK])
        rank = sb("rank", [HC, DB, NBLK])
        mx = sb("mx", [HC, 4, DB])
        bias4 = sb("bias4", [P, DB, 2])
        esum = sb("esum", [P, DB, 2])
        tot = sb("tot", [HC, DB, NBLK + 1])
        rinv = sb("rinv", [HC, DB])
        col = sb("col", [P, 16])

        ps = ctx.enter_context(nc.psum_tensor("ps_acc", [P, 2, 2, 512], F32))
        ps_a = ctx.enter_context(nc.psum_tensor("ps_a", [P, 2, 512], F32))
        ps_b = ctx.enter_context(nc.psum_tensor("ps_b", [P, 2, 512], F32))

        w_loaded = [sem(f"w_loaded{i}") for i in range(RING)]
        hi_ready = sem("hi_ready")
        lo_ready = sem("lo_ready")
        unit_used = sem("unit_used")
        acc_done = sem("acc_done")
        acc_free = sem("acc_free")
        act_ready = sem("act_ready")
        act_hi_done = sem("act_hi_done")
        sq_done = sem("sq_done")
        sq_added = sem("sq_added")
        ss_done = sem("ss_done")
        var_ready = sem("var_ready")
        root_done = sem("root_done")
        const_in = sem("const_in")
        x_loaded = [sem(f"x_loaded{i}") for i in range(4)]
        st_ready = sem("st_ready")
        st_copied = sem("st_copied")
        st_stored = [sem(f"st_stored{i}") for i in range(2)]
        st_free = sem("st_free")
        page_loaded = [sem(f"page_loaded{i}") for i in range(RING)]
        page_used = sem("page_used")
        q_zeroed = sem("q_zeroed")
        q_ready = sem("q_ready")
        scores_out = sem("scores_out")
        vt_done = sem("vt_done")
        vt_out = sem("vt_out")
        pe_s = sem("pe_s")
        dve_s = sem("dve_s")
        act_s = sem("act_s")
        pa_scores = sem("pa_scores")
        pa_max = sem("pa_max")
        pa_exp = sem("pa_exp")
        pa_norm = sem("pa_norm")
        pa_trans = sem("pa_trans")
        pa_copied = sem("pa_copied")
        pa_out = sem("pa_out")
        pa_stored = sem("pa_stored")
        pt_done = sem("pt_done")
        pt_out = sem("pt_out")
        new_out = sem("new_out")
        p_ready = sem("p_ready")
        pv_out = sem("pv_out")
        new_done = sem("new_done")
        ext_ready = sem("ext_ready")
        ext_stored = sem("ext_stored")
        hist_loaded = sem("hist_loaded")
        hist_placed = sem("hist_placed")
        pooled = sem("pooled")
        d_hi = sem("d_hi")
        d_ready = sem("d_ready")
        attn_ready = sem("attn_ready")
        mix_out = sem("mix_out")
        x_again = sem("x_again")
        par_loaded = sem("par_loaded")
        scaled = sem("scaled")
        x2_ready = sem("x2_ready")
        g_ready = sem("g_ready")
        g_hist = sem("g_hist")
        c_started = sem("c_started")
        c_ready = sem("c_ready")
        gelu_done = sem("gelu_done")
        f_ready = sem("f_ready")
        f_hi_done = sem("f_hi_done")
        f_split = sem("f_split")
        tails_out = sem("tails_out")
        rstd_ready = sem("rstd_ready")
        y_ready = sem("y_ready")
        out_done = sem("out_done")

        block = ctx.enter_context(nc.Block())

        def load_unit(sp, q, k, first=False):
            if not first:
                sp.wait_ge(lo_ready, 4 * q + k - RING + 1)
            u = 4 * q + k
            src = units[u] if isinstance(u, int) else units[bass.ds(u, 1)].rearrange("a p n -> p (a n)")
            sp.dma_start(w_raw[:, k % RING].rearrange("p a n -> p (a n)"), src).then_inc(w_loaded[k % RING], 16)

        def split_hi(act, q, k, first=False):
            s = k % RING
            act.wait_ge(w_loaded[s], 16 * (q + k // RING + 1))
            if not first:
                act.wait_ge(unit_used, 4 * q + k - RING + 1)
            act.activation(w_hi[:, s], w_raw[:, s], ACT.Copy).then_inc(hi_ready, 1)

        def split_lo(dve, q, k):
            s = k % RING
            dve.wait_ge(hi_ready, 4 * q + k + 1)
            dve.tensor_tensor(w_lo[:, s], w_raw[:, s], w_hi[:, s].bitcast(F32), ALU.subtract).then_inc(lo_ready, 1)

        def tile_done(eng, G, mt, q, k):
            if mt == 0:
                eng.wait_ge(acc_done, G + 1)
            else:
                eng.wait_ge(unit_used, 4 * q + k + 1)

        def half(ap, i):
            return ap[:, i * HN:(i + 1) * HN]

        def banks(mt, odd=0):
            return (ps_a, ps_b)[mt] if odd else ps[:, mt]

        def bank(mt, odd=0):
            return banks(mt, odd)[:, :, 0:HN]

        def two(ap):
            return ap.rearrange("p (a n) -> p a n", a=2)

        @block.sync
        def _(sp):
            pg = [sp.alloc_register(f"page{i}") for i in range(8)]

            def load_x(i):
                sp.dma_start(x_in[:, 4 * i:4 * i + 4], xT[:, 4 * i:4 * i + 4]).then_inc(x_loaded[i], 16)

            def load_page(cache, slot, reg, used):
                if used is not None:
                    sp.wait_ge(page_used, used)
                i = sp.snap(reg, min_val=0, max_val=N_PHYS - 1)
                sp.dma_start(pages[:, slot], cache[bass.ds(i, 1)].rearrange("a p n -> p (a n)"))\
                    .then_inc(page_loaded[slot], 16)

            sp.dma_start(gain[:], gains).then_inc(const_in, 16)
            load_x(0)
            load_unit(sp, 0, 0, first=True)
            load_unit(sp, 0, 1, first=True)
            load_x(1)
            load_unit(sp, 0, 2, first=True)
            load_x(2)
            load_unit(sp, 0, 3, first=True)
            load_x(3)
            sp.dma_start(cst[:], consts).then_inc(const_in, 16)
            sp.dma_start(shared[0:32], rope_tab).then_inc(const_in, 16)
            with sp.Fori(0, 4) as g:
                for u in range(8):
                    load_unit(sp, 2 * g, u + RING)
            with sp.Fori(4, 12) as g:
                for u in range(8):
                    if u % 4 == 0:
                        sp.load(pg, table[bass.ds(2 * g - 8 + u // 4, 1), :])
                    load_unit(sp, 2 * g, u + RING)
                    for i in (2 * u, 2 * u + 1):
                        load_page(kcache, i % RING, pg[i % 8], 16 * g - 64 + i + 1)
            with sp.Fori(12, 16) as g:
                for u in range(8):
                    if u % 2 == 0:
                        sp.load(pg, table[bass.ds(4 * g - 48 + u // 2, 1), :])
                    load_unit(sp, 2 * g, u + RING)
                    for i in range(4 * u, 4 * u + 4):
                        load_page(vcache, i % RING, pg[i % 8], 32 * g - 384 + 128 + i + 1)
            for k in range(4):
                load_unit(sp, Q_POOL, k + RING)
            sp.wait_ge(act_ready, 2 * KT)
            sp.wait_ge(new_done, 1)
            for i in range(4):
                sp.dma_start(x2[:, 4 * i:4 * i + 4], xT[:, 4 * i:4 * i + 4]).then_inc(x_again, 16)
            sp.dma_start(par, conv_par).then_inc(par_loaded, 16)
            with sp.Fori(0, 8) as g:
                for u in range(8):
                    load_unit(sp, 2 * g + Q_OUT, u + RING)
            with sp.Fori(0, NCH - 1) as c:
                for k in range(4 * Q_CH):
                    load_unit(sp, c * Q_CH + Q_FF, k + RING)
            for k in range(4 * Q_CH - RING):
                load_unit(sp, (NCH - 1) * Q_CH + Q_FF, k + RING)

        @block.scalar
        def _(act):
            def act_tile(kt, src, g, hi=None):
                act.activation(act_hi[:, kt], src, ACT.Copy, scale=g[:, kt:kt + 1]).then_inc(act_hi_done, 1)

            def squares(src, s, freed):
                if freed is not None:
                    act.wait_ge(sq_added, freed)
                act.activation(sq[:, s], src, ACT.Square).then_inc(sq_done, 1)

            def root(n):
                act.wait_ge(var_ready, n)
                act.activation(rstd[:, :], tmp, ACT.Sqrt).then_inc(root_done, 1)

            act.sem_inc(scores_out, 2)
            act.sem_inc(vt_out, 2)
            act.sem_inc(pv_out, 2)
            act.sem_inc(st_free, 2)

            def prep(kt):
                if kt == 0:
                    act.wait_ge(const_in, 16)
                if kt % 4 == 0:
                    act.wait_ge(x_loaded[kt // 4], 16)
                act_tile(kt, x_in[:, kt], g_pre)
                squares(x_in[:, kt], kt % 2, kt - 1 if kt >= 2 else None)

            split_hi(act, 0, 0, first=True)
            prep(0)
            prep(1)
            split_hi(act, 0, 1, first=True)
            split_hi(act, 0, 2, first=True)
            for u in range(8):
                split_hi(act, 0, u + LEAD, first=u + LEAD < RING)
                if u < 7:
                    prep(2 * u + 2)
                    prep(2 * u + 3)
            root(1)

            def copy_heads(dst, g0, g):
                for mt in range(2):
                    act.wait_ge(st_ready, 2 * g + mt + 1)
                    h = 2 * (g - g0) + mt
                    out = dst[:, h] if isinstance(h, int) else dst[:, bass.ds(h, 1)].rearrange("p a n -> p (a n)")
                    act.activation(out, stage[:, mt], ACT.Copy).then_inc(st_copied, 1)

            copy_heads(qT, 0, 0)
            with act.Fori(1, 4) as g:
                for u in range(8):
                    split_hi(act, 2 * g, u + LEAD)
                copy_heads(qT, 0, g)

            def load_q(b):
                act.wait_ge(page_used, 16 * b + RING)
                src = qT[:, :, bass.ds(b * DL + SEQ, DL)]
                act.activation(q_blk[:, :].rearrange("p (h l) -> p h l", h=NH)[:, :, 0:DL], src, ACT.Copy)\
                    .then_inc(q_ready, 1)

            def store_scores(b, quad):
                act.wait_ge(page_used, 16 * b + 4 * quad + 4 + RING)
                act.activation(s_all[quad * HC:(quad + 1) * HC, bass.ds(b, 1)].rearrange("p a n -> p (a n)"),
                               ps_a[0:HC, quad % 2, :], ACT.Copy).then_inc(scores_out, 1)

            def kv_group(g):
                load_q(g - 4)
                for u in range(8):
                    split_hi(act, 2 * g, u + LEAD)
                    if u in (2, 4, 6):
                        store_scores(g - 4, u // 2 - 1)

            with act.Fori(4, 8) as g:
                act.wait_ge(st_copied, 8)
                act.wait_ge(q_zeroed, 1)
                kv_group(g)
                copy_heads(kT, 4, g)
                store_scores(g - 4, 3)
            with act.Fori(8, 12) as g:
                kv_group(g)
                for mt in range(2):
                    act.wait_ge(st_ready, 2 * g + mt + 1)
                    act.activation(v_dec[:, :, bass.ds((2 * g - 16 + mt) * DL, DL)],
                                   stage[:, mt, SEQ:NT].rearrange("p (b l) -> p b l", b=DB), ACT.Copy)\
                        .then_inc(st_copied, 1)
                store_scores(g - 4, 3)
                for mt in range(2):
                    act.wait_ge(vt_done, 2 * g - 15 + mt)
                    act.activation(v_tok[:, bass.ds(2 * g - 16 + mt, 1)].rearrange("p a t d -> p (a t d)"),
                                   ps_b[:, mt, :], ACT.Copy).then_inc(vt_out, 1)

            act.activation(q_dec[:, :, :].rearrange("p b (h l) -> p h b l", h=NH),
                           qT[:, :, SEQ:NT].rearrange("p h (b l) -> p h b l", b=DB), ACT.Copy).then_inc(q_ready, 1)
            act.wait_ge(pe_s, 2)
            act.activation(v_new.rearrange("p (a b) d -> p a (b d)", a=2), ps[0:HC, 1], ACT.Copy).then_inc(new_out, 1)

            def decode_exp(b):
                if b == 0:
                    act.wait_ge(dve_s, 2)
                for k in range(2):
                    c = s_all[:, b, k * 256:(k + 1) * 256]
                    act.activation(c, c, ACT.Exp, scale=SCALE, bias=bias4[:, b, k:k + 1],
                                   accum_out=esum[:, b, k:k + 1])
                act.activation(p_new[:, b], p_new[:, b], ACT.Exp, scale=SCALE, bias=mx[:, 3, b:b + 1],
                               accum_out=tot[:, b, NBLK:NBLK + 1]).then_inc(act_s, 1)

            act.wait_ge(st_free, 2 * 8 + 2)
            for h in range(NH):
                for qi in range(4):
                    t = 4 * h + qi
                    n = (qi + 1) * P
                    act.wait_ge(pa_max, t + 1)
                    if t >= 2:
                        act.wait_ge(pa_trans, t - 1)
                    act.activation(prob[:, t % 2, 0:n], ps_a[:, t % 2, 0:n], ACT.Exp, scale=SCALE,
                                   bias=col[:, t % 2:t % 2 + 1], accum_out=col[:, 2 + t % 2:3 + t % 2])\
                        .then_inc(pa_exp, 1)
                    act.wait_ge(pa_trans, t + 1)
                    if qi == 0 and h:
                        act.wait_ge(pa_out, h)
                    act.activation(probT[:, 0:qi + 1, qi * P:(qi + 1) * P],
                                   ps_b[:, t % 2, 0:n].rearrange("p (k n) -> p k n", k=qi + 1), ACT.Copy)\
                        .then_inc(pa_copied, 1)
                    if qi == 1:
                        decode_exp(h)
                act.wait_ge(pa_out, h + 1)
                act.activation(qT[:, h, 0:SEQ], ps[:, 0, h % 2, :], ACT.Copy).then_inc(pa_stored, 1)
            act.wait_ge(pe_s, 3)
            act.activation(p_newT.rearrange("p b n -> p (b n)"), ps_a[0:HC, 0, 0:DB * HC], ACT.Copy)\
                .then_inc(new_out, 1)

            act.wait_ge(pt_out, DB)
            act.wait_ge(dve_s, 3)

            def store_values(i, s):
                act.wait_ge(hist_placed, 1)
                act.wait_ge(page_used, 64 * i + 16 * s + 144 + RING)
                act.activation(o_all[s * HC:(s + 1) * HC, bass.ds(i, 1)].rearrange("p a n -> p (a n)"),
                               (ps_a, ps_b)[s % 2][0:HC, :, :].rearrange("p a n -> p (a n)"), ACT.Copy,
                               scale=rinv[:, bass.ds(4 * i + s, 1)]).then_inc(pv_out, 1)

            with act.Fori(0, 2) as i:
                for s in range(4):
                    act.wait_ge(page_used, 64 * i + 16 * s + 112 + RING)
                    act.activation(p_seq[:, s % 2], s_all[:, bass.ds(4 * i + s, 1)].rearrange("p a n -> p (a n)"),
                                   ACT.Copy).then_inc(p_ready, 1)
                    for u in range(4 * s, 4 * s + 4):
                        split_hi(act, 4 * i + 2 * 12, u + LEAD)
                    store_values(i, s)
            act.wait_ge(new_done, 1)
            act.activation(qT[:, :, SEQ:NT], ps_a[:, 0, 0:DB * HC].rearrange("p (h n) -> p h n", h=NH), ACT.Copy)\
                .then_inc(attn_ready, 1)

            def pool_hi(j):
                act.wait_ge(pooled, j + 1)
                if j == 0:
                    act.wait_ge(page_used, 2 * DB * PAGES + RING)
                if j >= 2:
                    act.wait_ge(unit_used, 4 * Q_POOL + j - 1)
                f = 2 * (j % 2)
                act.activation(f_hi[:, f:f + 2, 0:SEQ], ext[:, 2 * j:2 * j + 2, HIST:HIST + SEQ], ACT.Copy)
                for t in range(2):
                    i = act.activation(f_hi[:, f + t, SEQ:NT].rearrange("p (b l) -> p b l", b=DB),
                                       ext_s(ext[:, 2 * j + t]), ACT.Copy)
                i.then_inc(d_hi, 1)

            def ext_s(row):
                return row[:, HIST + SEQ:EXT].rearrange("p (b n) -> p b n", b=DB)[:, :, HIST:SEG]

            for j in range(4):
                split_hi(act, Q_POOL, j + LEAD)
                pool_hi(j)
                if j == 0:
                    act.wait_ge(unit_used, 4 * Q_POOL)
                    for h in range(NH):
                        if h == 0:
                            act.wait_ge(attn_ready, 1)
                        act.activation(act_hi[:, h], qT[:, h], ACT.Copy).then_inc(act_hi_done, 1)
                for mt in range(2):
                    tile_done(act, G_POOL + j, mt, Q_POOL, j)
                    t = NH + 2 * j + mt
                    act.activation(two(act_hi[:, t]), bank(mt), ACT.Copy, scale=pscale[:, 2 * j + mt:2 * j + mt + 1])\
                        .then_inc(act_hi_done, 1)

            def mix_squares(g):
                for mt in range(2):
                    act.wait_ge(mix_out, 2 * g + mt + 1)
                    m = 2 * g + mt
                    act.wait_ge(sq_added, KT - 1 + m)
                    act.activation(sq[:, mt], tile_of(acc, m), ACT.Square).then_inc(sq_done, 1)

            def tile_of(t, m):
                return t[:, m] if isinstance(m, int) else t[:, bass.ds(m, 1)].rearrange("p a n -> p (a n)")

            with act.Fori(0, 8) as g:
                for u in range(8):
                    split_hi(act, 2 * g + Q_OUT, u + LEAD)
                mix_squares(g)
            root(2)

            def prep2(kt):
                act.wait_ge(x2_ready, kt + 1)
                act_tile(kt, x2[:, kt], g_fpre)
                squares(x2[:, kt], kt % 2, 2 * KT + kt - 1)

            def ff_gate(g, F):
                def p_(i):
                    if isinstance(F, int):
                        return par[:, F, i:i + 1]
                    return par[:, bass.ds(F, 1), i:i + 1].rearrange("p a n -> p (a n)")
                act.wait_ge(g_ready, F + 1)
                act.activation(conv[:, 2:CEXT], g_ext[:, 2:CEXT], ACT.Identity, scale=p_(2), bias=p_(3))\
                    .then_inc(c_started, 1)
                act.wait_ge(c_ready, F + 1)
                act.activation(conv[:, 2:CEXT], conv[:, 2:CEXT], ACT.Gelu_apprx_tanh).then_inc(gelu_done, 1)

            def f_part(F, j):
                act.wait_ge(f_ready, F + 1)
                act.activation(tile_of(f_hi, j), f_buf, ACT.Copy).then_inc(f_hi_done, 1)

            def chunk(c, first=False, last=False):
                q0 = c * Q_CH + Q_FF
                g0 = c * G_CH + G_FF

                def gate_group(j, prepare=False):
                    for u in range(8):
                        split_hi(act, 2 * j + q0, u + LEAD)
                        if prepare and u < 7:
                            prep2(2 * u + 2)
                            prep2(2 * u + 3)
                    if prepare:
                        root(3)
                    F = c * CH + j
                    ff_gate(j + g0, F)
                    f_part(F, j)
                if first:
                    prep2(0)
                    prep2(1)
                    gate_group(0, prepare=True)
                with act.Fori(1 if first else 0, CH) as j:
                    gate_group(j)
                with act.Fori(0, 3 if last else 4) as d:
                    for k in range(4):
                        split_hi(act, d + q0 + 2 * CH, k + LEAD)
                    if last:
                        for i in range(4):
                            last_squares(4 * d + i, i % 2)
                if last:
                    split_hi(act, q0 + 2 * CH + 3, LEAD)
                    for i in range(4):
                        last_squares(12 + i, i % 2)

            def last_squares(m, s):
                act.wait_ge(mix_out, m + KT + 1)
                act.wait_ge(tails_out, 1)
                act.wait_ge(sq_added, m + 3 * KT - 1)
                act.activation(sq[:, s], tile_of(acc, m), ACT.Square).then_inc(sq_done, 1)

            chunk(0, first=True)
            with act.Fori(1, NCH - 1) as c:
                chunk(c)
            chunk(NCH - 1, last=True)
            root(4)

        @block.tensor
        def _(pe):
            def group(G, q, nu, hi, lo, ready=None, after=None, k0=0, first=False):
                for u in range(nu):
                    k = k0 + u
                    pe.wait_ge(lo_ready, 4 * q + k + 1)
                    if ready is not None:
                        pe.wait_ge(*ready(u))
                    s = k % RING
                    for mt in range(2):
                        if u == 0 and not first:
                            pe.wait_ge(acc_free, 2 * G + mt - 1)
                        for i in range(2):
                            kt = 2 * u + i
                            cols = slice(mt * P, (mt + 1) * P)
                            for w, a in ((w_hi, hi), (w_hi, lo), (w_lo, hi)):
                                for n in range(2):
                                    mm = pe.matmul(ps[:, mt, n, 0:HN], w[:, s, i, cols], half(a[:, kt], n),
                                                   start=kt == 0 and w is w_hi and a is hi,
                                                   stop=kt == 2 * nu - 1 and w is w_lo)
                        if u == nu - 1 and mt == 0:
                            mm.then_inc(acc_done, 1)
                    mm.then_inc(unit_used, 1)
                    if after is not None:
                        after(u)

            def ff_unit(G, q, k, u, nu, hi, lo, odd, ready, prev=2):
                pe.wait_ge(lo_ready, 4 * q + k + 1)
                s = k % RING
                for i in range(2):
                    kt = 2 * u + i
                    if ready is not None:
                        pe.wait_ge(*ready(kt))
                    for mt in range(2):
                        if kt == 0:
                            pe.wait_ge(acc_free, 2 * G + mt + 1 - 2 * prev)
                        cols = slice(mt * P, (mt + 1) * P)
                        for w, a in ((w_hi, hi), (w_hi, lo), (w_lo, hi)):
                            for n in range(2):
                                mm = pe.matmul(banks(mt, odd)[:, n, 0:HN], w[:, s, i, cols], half(a[:, kt], n),
                                               start=kt == 0 and w is w_hi and a is hi,
                                               stop=kt == 2 * nu - 1 and w is w_lo)
                        if kt == 2 * nu - 1 and mt == 0:
                            mm.then_inc(acc_done, 1)
                mm.then_inc(unit_used, 1)

            def sum_squares(n):
                pe.wait_ge(sq_added, n)
                for i in range(2):
                    mm = pe.matmul(ps_a[:, i, 0:HN], ones, half(sq_sum, i), start=True, stop=True)
                mm.then_inc(ss_done, 1)

            def ready1(u):
                return act_ready, 2 * u + 2

            pe.wait_ge(const_in, 48)
            group(0, 0, 8, act_hi, act_lo, ready1, first=True)
            sum_squares(KT)
            with pe.Fori(1, 4) as g:
                group(g, 2 * g, 8, act_hi, act_lo)

            def scores(g):
                b = g - 4

                def after(u):
                    quad, s = u // 2, 2 * (u % 2)
                    for i in range(2):
                        pe.wait_ge(page_loaded[s + i], (b * 4 + quad + 1) * 16)
                    if u == 0:
                        pe.wait_ge(q_ready, b + 1)
                    if s == 0:
                        pe.wait_ge(scores_out, 4 * b + quad + 1)
                    for h in range(NH):
                        mm = pe.matmul(ps_a[0:HC, quad % 2, s * P:(s + 2) * P], q_blk[:, h * HC:(h + 1) * HC],
                                       pages[:, s:s + 2, h * P:(h + 1) * P], start=h == 0, stop=h == NH - 1)
                    mm.then_inc(page_used, 2)
                return after

            pe.sem_inc(page_used, RING)
            with pe.Fori(4, 8) as g:
                group(g, 2 * g, 8, act_hi, act_lo, after=scores(g))
            with pe.Fori(8, 12) as g:
                group(g, 2 * g, 8, act_hi, act_lo, after=scores(g))
                pe.wait_ge(vt_out, 2 * g - 16 + 2)
                for mt in range(2):
                    pe.wait_ge(st_ready, 2 * g + mt + 1)
                    for t in range(4):
                        mm = pe.transpose(ps_b[:, mt, t * P:(t + 1) * P], stage[:, mt, t * P:(t + 1) * P], ident)
                    mm.then_inc(vt_done, 1)

            pe.wait_ge(vt_out, 10)
            pe.wait_ge(st_copied, 24)
            pe.wait_ge(q_ready, DB + 1)
            for b in range(DB):
                new = slice(SEQ + b * DL, SEQ + (b + 1) * DL)
                mm = pe.matmul(ps_b[0:HC, 0, b * HC:(b + 1) * HC], q_dec[:, b], kT[:, :, new],
                               start=True, stop=True)
            mm.then_inc(pe_s, 1)
            pe.wait_ge(acc_free, 24)
            for b in range(DB):
                mm = pe.transpose(ps[0:HC, 1, b // 4, (b % 4) * P:(b % 4 + 1) * P], v_dec[:, b],
                                  ident)
            mm.then_inc(pe_s, 1)

            def prompt_scores(t):
                h, qi = divmod(t, 4)
                n = (qi + 1) * P
                if t >= 2:
                    pe.wait_ge(pa_exp, t - 1)
                q = qT[:, h, qi * P:(qi + 1) * P]
                if qi:
                    pe.matmul(ps_a[:, t % 2, 0:n - P], q, kT[:, h, 0:n - P], start=True, stop=True)
                pe.matmul(ps_a[:, t % 2, n - P:n], q, kT[:, h, n - P:n], start=True, stop=False)
                pe.matmul(ps_a[:, t % 2, n - P:n], ident, causal, start=False, stop=True).then_inc(pa_scores, 1)

            def decode_transposes(b):
                pe.wait_ge(act_s, b + 1)
                if b == 0:
                    pe.wait_ge(new_out, 1)
                if b >= 2:
                    pe.wait_ge(pt_out, b - 1)
                for c in range(4):
                    mm = pe.transpose(ps[:, 1, b % 2, c * P:(c + 1) * P], s_all[:, b, c * P:(c + 1) * P], ident)
                mm.then_inc(pt_done, 1)

            pe.wait_ge(scores_out, 4 * DB + 2)
            prompt_scores(0)
            for h in range(NH):
                for qi in range(4):
                    t = 4 * h + qi
                    if t + 1 < 4 * NH:
                        prompt_scores(t + 1)
                    pe.wait_ge(pa_norm, t + 1)
                    if t == 0:
                        pe.wait_ge(dve_s, 1)
                    if t >= 2:
                        pe.wait_ge(pa_copied, t - 1)
                    for kj in range(qi + 1):
                        mm = pe.transpose(ps_b[:, t % 2, kj * P:(kj + 1) * P], prob[:, t % 2, kj * P:(kj + 1) * P],
                                          ident)
                    mm.then_inc(pa_trans, 1)
                pe.wait_ge(pa_copied, 4 * h + 4)
                if h >= 2:
                    pe.wait_ge(pa_stored, h - 1)
                for kj in range(4):
                    mm = pe.matmul(ps[:, 0, h % 2, kj * P:SEQ], v_tok[:, h, kj], probT[:, kj, kj * P:SEQ],
                                   start=kj == 0, stop=kj == 3)
                mm.then_inc(pa_out, 1)
                decode_transposes(h)
            pe.wait_ge(dve_s, 3)
            for b in range(DB):
                mm = pe.transpose(ps_a[0:HC, 0, b * HC:(b + 1) * HC], p_new[:, b], ident[0:HC, 0:HC])
            mm.then_inc(pe_s, 1)
            pe.wait_ge(new_out, 2)
            pe.wait_ge(pt_out, DB)
            pe.wait_ge(pa_stored, NH)

            with pe.Fori(0, 2) as i:
                def values(s, u):
                    o = (ps_a, ps_b)[s % 2]
                    for slot in range(RING):
                        pg = 4 * u + slot
                        pe.wait_ge(page_loaded[slot], (16 * i + 4 * s + 33 + u) * 16)
                        if pg == 0:
                            pe.wait_ge(p_ready, 4 * i + s + 1)
                            pe.wait_ge(pv_out, 4 * i + s + 1)
                        c = ((pg % 4) * 4 + pg // 4) * HC
                        for n in range(2):
                            mm = pe.matmul(o[0:HC, n, :], p_seq[:, s % 2, c:c + HC],
                                           pages[:, slot, n * 512:(n + 1) * 512], start=pg == 0, stop=pg == PAGES - 1)
                        mm.then_inc(page_used, 1)
                for half_turn in range(2):
                    group(2 * i + 12 + half_turn, 4 * i + 24 + 2 * half_turn, 8, act_hi, act_lo,
                          after=lambda u, s=2 * half_turn: values(s + u // 4, u % 4))
            pe.wait_ge(pv_out, DB + 2)
            for a in range(2):
                for h in range(NH):
                    pe.matmul(ps_a[:, 0, h * HC + a * 16:h * HC + (a + 1) * 16], o_all[:, a, h * P:(h + 1) * P],
                              ident.rearrange("p (b n) -> p b n", b=4)[:, :, h * DL:(h + 1) * DL],
                              start=a == 0 and h == 0, stop=False, skip_group_check=True)
            for b in range(DB):
                mm = pe.matmul(ps_a[:, 0, 0:DB * HC].rearrange("p (h n) -> p h n", h=NH)[:, :, b * DL:(b + 1) * DL],
                               v_new[:, b], p_newT[:, b], start=False, stop=True, skip_group_check=True)
            mm.then_inc(new_done, 1)

            for j in range(4):
                pe.wait_ge(d_ready, j + 1)
                f = 2 * (j % 2)
                group(G_POOL + j, Q_POOL, 1, f_hi[:, f:f + 2], f_lo[:, f:f + 2], k0=j)

            def ready2(u):
                return act_ready, KT + 2 * u + 2

            with pe.Fori(0, 8) as g:
                group(g + G_OUT, 2 * g + Q_OUT, 8, act_hi, act_lo, ready2)
            sum_squares(2 * KT)

            def ready3(u):
                return act_ready, 2 * KT + 2 * u + 2

            def gate_up(G, q, odd, ready=None, prev=2):
                for u in range(8):
                    ff_unit(G, q, u, u, 8, act_hi, act_lo, odd, ready, prev)

            def chunk(c, first=False):
                q0 = c * Q_CH + Q_FF
                g0 = c * G_CH + G_FF
                if first:
                    gate_up(g0, q0, 0, lambda kt: (act_ready, 2 * KT + kt + 1), prev=1)
                    sum_squares(3 * KT)
                    pe.wait_ge(var_ready, 3)
                    gate_up(g0 + 1, q0 + 2, 1)
                with pe.Fori(1 if first else 0, CH // 2) as j:
                    for odd in range(2):
                        gate_up(2 * j + g0 + odd, 4 * j + q0 + 2 * odd, odd)

                def f_ready(kt):
                    return f_split, c * CH + kt + 1
                with pe.Fori(0, 4) as d:
                    for k in range(4):
                        ff_unit(2 * d + g0 + CH + k % 2, d + q0 + 2 * CH, k, k // 2, 2, f_hi, f_lo, k % 2,
                                f_ready if k % 2 == 0 else None)

            chunk(0, first=True)
            with pe.Fori(1, NCH) as c:
                chunk(c)
            sum_squares(4 * KT)

        @block.vector
        def _(dve):
            def tile_of(t, m):
                return t[:, m] if isinstance(m, int) else t[:, bass.ds(m, 1)].rearrange("p a n -> p (a n)")

            def add_square(n, s, start=False):
                dve.wait_ge(sq_done, n)
                if start:
                    return dve.tensor_copy(sq_sum, sq[:, s]).then_inc(sq_added, 1)
                dve.drain()
                return dve.tensor_tensor(sq_sum, sq_sum, sq[:, s], ALU.add).then_inc(sq_added, 1)

            def root_mean(n):
                dve.wait_ge(ss_done, n)
                dve.tensor_scalar(two(tmp), ps_a[:, :, 0:HN], 1.0 / D, EPS, ALU.mult, ALU.add).then_inc(var_ready, 1)
                dve.wait_ge(root_done, n)
                dve.reciprocal(rstd[:, :], rstd[:, :])
                dve.drain()
                dve.tensor_tensor(sq[:, 0], rstd[:, :], rstd[:, :], ALU.mult)
                dve.drain()
                dve.scalar_tensor_tensor(sq[:, 0], sq[:, 0], -0.5, tmp, ALU.mult, ALU.mult)
                dve.drain()
                dve.scalar_tensor_tensor(rstd[:, :], sq[:, 0], 1.5, rstd[:, :], ALU.add, ALU.mult)
                dve.drain().then_inc(rstd_ready, 1)

            def prep(kt, src, g, n0):
                dve.wait_ge(act_hi_done, n0 + kt + 1)
                dve.scalar_tensor_tensor(act_lo[:, kt], src[:, kt], g[:, kt:kt + 1], act_hi[:, kt].bitcast(F32),
                                         ALU.mult, ALU.subtract).then_inc(act_ready, 1)

            split_lo(dve, 0, 0)
            for kt in range(2):
                prep(kt, x_in, g_pre, 0)
                add_square(kt + 1, kt, start=kt == 0)
            split_lo(dve, 0, 1)
            split_lo(dve, 0, 2)
            for u in range(8):
                split_lo(dve, 0, u + LEAD)
                for kt in (2 * u + 2, 2 * u + 3):
                    if kt < KT:
                        prep(kt, x_in, g_pre, 0)
                        add_square(kt + 1, kt % 2)
            root_mean(1)

            def to_stage(g, mt):
                tile_done(dve, g, mt, 2 * g, 7)
                dve.tensor_tensor(two(stage[:, mt]), bank(mt), two(rstd[:, :]), ALU.mult).then_inc(acc_free, 1)

            def rope(mt):
                x = stage[0:32, mt]
                dve.drain()
                dve.stream_shuffle(swap, x, [(i + 16) % 32 for i in range(32)])
                dve.drain()
                dve.tensor_tensor(x, x, cos_t, ALU.mult)
                dve.tensor_tensor(swap, swap, sin_t, ALU.mult)
                dve.drain()
                dve.tensor_tensor(x, x, swap, ALU.add).then_inc(st_ready, 1)

            def heads(g):
                for mt in range(2):
                    to_stage(g, mt)
                for mt in range(2):
                    rope(mt)

            dve.wait_ge(const_in, 48)
            heads(0)
            with dve.Fori(1, 4) as g:
                for u in range(8):
                    split_lo(dve, 2 * g, u + LEAD)
                dve.wait_ge(st_copied, 2 * g)
                heads(g)

            def block_stats(b, quad):
                dve.wait_ge(scores_out, 4 * b + quad + 3)
                src = s_all[quad * HC:(quad + 1) * HC, bass.ds(b, 1)].rearrange("p a (k n) -> p (a k) n", k=2)
                for dst, op in ((gate, ALU.add), (bmax, ALU.max)):
                    dve.tensor_reduce(dst[:, bass.ds(b, 1), 2 * quad:2 * quad + 2].rearrange("p a k -> p (a k)"), src,
                                      AX.X, op)

            def kv_splits(g):
                for u in range(8):
                    split_lo(dve, 2 * g, u + LEAD)
                    if u in (2, 4, 6):
                        block_stats(g - 4, u // 2 - 1)

            with dve.Fori(4, 8) as g:
                kv_splits(g)
                dve.wait_ge(st_copied, 2 * g)
                dve.wait_ge(st_free, 2 * g - 6)
                heads(g)
                block_stats(g - 4, 3)
            with dve.Fori(8, 12) as g:
                kv_splits(g)
                dve.wait_ge(st_copied, 2 * g)
                dve.wait_ge(st_free, 2 * g - 6)
                for mt in range(2):
                    tile_done(dve, g, mt, 2 * g, 7)
                    dve.tensor_tensor(two(stage[:, mt]), bank(mt), two(rstd[:, :]), ALU.mult).then_inc(acc_free, 1)
                    dve.drain().then_inc(st_ready, 1)
                block_stats(g - 4, 3)

            dve.wait_ge(pe_s, 1)
            dve.tensor_tensor(p_new[:, :, :], ps_b[0:HC, 0, 0:DB * HC].rearrange("p (b n) -> p b n", b=DB),
                              new_mask.unsqueeze(1).to_broadcast([HC, DB, HC]), ALU.add).then_inc(dve_s, 1)
            dve.drain()
            gj = gate[:, :, :].unsqueeze(2).to_broadcast([HC, DB, NBLK, NBLK])
            gi = gate[:, :, :].unsqueeze(3).to_broadcast([HC, DB, NBLK, NBLK])
            above = shared[0:HC, 0, 0:512].rearrange("p (b i j) -> p b i j", b=DB, i=NBLK)
            tied = shared[0:HC, 1, 0:512].rearrange("p (b i j) -> p b i j", b=DB, i=NBLK)
            dve.tensor_tensor(above, gj, gi, ALU.is_gt)
            dve.tensor_tensor(tied, gj, gi, ALU.is_equal)
            dve.drain()
            dve.tensor_tensor(tied, tied, below.unsqueeze(1).to_broadcast([HC, DB, NBLK, NBLK]), ALU.mult)
            dve.tensor_reduce(mx[:, 0], p_new[:, :, :], AX.X, ALU.max)
            dve.drain()
            dve.tensor_tensor(above, above, tied, ALU.add)
            dve.drain()
            dve.tensor_reduce(rank[:, :, :], above, AX.X, ALU.add)
            dve.drain()
            dve.tensor_scalar(rank[:, :, :], rank[:, :, :], float(TOPK), NEG, ALU.is_ge, ALU.mult)
            dve.drain()
            dve.tensor_tensor(bmax[:, :, :], bmax[:, :, :], rank[:, :, :], ALU.add)
            dve.drain()
            dve.tensor_reduce(mx[:, 1], bmax[:, :, :], AX.X, ALU.max)
            dve.drain()
            dve.tensor_tensor(mx[:, 2], mx[:, 0], mx[:, 1], ALU.max)
            dve.drain()
            dve.tensor_scalar(mx[:, 3], mx[:, 2], -SCALE, None, ALU.mult)
            dve.drain()
            dve.tensor_tensor(rank[:, :, :], rank[:, :, :], mx[:, 3].unsqueeze(2).to_broadcast([HC, DB, NBLK]), ALU.add)
            dve.drain()
            for quad in range(4):
                o = dve.tensor_copy(bias4[quad * HC:(quad + 1) * HC], rank[:, :, 2 * quad:2 * quad + 2])
            o.then_inc(dve_s, 1)

            def row_max(t):
                n = (t % 4 + 1) * P
                dve.wait_ge(pa_scores, t + 1)
                dve.tensor_reduce(col[:, 10 + t % 2:11 + t % 2], ps_a[:, t % 2, 0:n], AX.X, ALU.max)
                dve.drain()
                dve.tensor_scalar(col[:, t % 2:t % 2 + 1], col[:, 10 + t % 2:11 + t % 2], -SCALE, None, ALU.mult).then_inc(pa_max, 1)

            def decode_back(b):
                dve.wait_ge(pt_done, b + 1)
                dve.tensor_copy(s_all[:, b], ps[:, 1, b % 2, :]).then_inc(pt_out, 1)

            row_max(0)
            for t in range(4 * NH):
                if t + 1 < 4 * NH:
                    row_max(t + 1)
                n = (t % 4 + 1) * P
                dve.wait_ge(pa_exp, t + 1)
                dve.reciprocal(col[:, 12 + t % 2:13 + t % 2], col[:, 2 + t % 2:3 + t % 2])
                dve.drain()
                dve.tensor_scalar(prob[:, t % 2, 0:n], prob[:, t % 2, 0:n], col[:, 12 + t % 2:13 + t % 2], None,
                                  ALU.mult).then_inc(pa_norm, 1)
                if t % 4 == 2 and t > 4:
                    decode_back(t // 4 - 1)
            dve.wait_ge(act_s, DB)
            for quad in range(4):
                dve.tensor_copy(tot[:, :, 2 * quad:2 * quad + 2], esum[quad * HC:(quad + 1) * HC])
            dve.drain()
            dve.tensor_reduce(rinv[:, :], tot[:, :, :], AX.X, ALU.add)
            dve.drain()
            dve.reciprocal(rinv[:, :], rinv[:, :])
            dve.drain()
            dve.tensor_tensor(p_new[:, :, :], p_new[:, :, :], rinv[:, :].unsqueeze(2).to_broadcast([HC, DB, HC]),
                              ALU.mult).then_inc(dve_s, 1)
            decode_back(NH - 1)

            def ext_s(row):
                return row[:, HIST + SEQ:EXT].rearrange("p (b n) -> p b n", b=DB)[:, :, HIST:SEG]

            def samples(ap):
                return ap[:, SEQ:NT].rearrange("p (b l) -> p b l", b=DB)

            def ext_row(t, mt, g):
                tile_done(dve, g, mt, 2 * g, 7)
                row = ext[:, t]
                dve.tensor_tensor(row[:, HIST:HIST + HN], ps[:, mt, 0, 0:HN], rstd[:, 0:HN], ALU.mult)
                dve.tensor_tensor(row[:, HIST + HN:HIST + SEQ], ps[:, mt, 1, 0:SEQ - HN], rstd[:, HN:SEQ], ALU.mult)
                dve.tensor_tensor(ext_s(row), ps[:, mt, 1, SEQ - HN:HN].rearrange("p (b l) -> p b l", b=DB),
                                  samples(rstd), ALU.mult).then_inc(acc_free, 1)
                dve.drain().then_inc(ext_ready, 1)

            def pool(j):
                w = WINDOWS[j]
                dve.wait_ge(hist_placed, 1)
                rows, src, s, step = ext[:, 2 * j:2 * j + 2], None, 0, 1
                src = rows
                while step < w:
                    lo = 2 * step - 1
                    dst = win[:, s]
                    dve.tensor_tensor(dst[:, :, lo:EXT], src[:, :, lo:EXT], src[:, :, lo - step:EXT - step], ALU.add)
                    dve.drain()
                    src, s, step = dst, 1 - s, 2 * step
                dve.tensor_tensor(src[:, :, HIST:HIST + 16], src[:, :, HIST:HIST + 16],
                                  corr[:, j:j + 1, :].to_broadcast([P, 2, 16]), ALU.mult)
                dve.drain()
                dve.wait_ge(ext_stored, 32 * (j + 1))
                dve.scalar_tensor_tensor(rows[:, :, HIST:EXT], src[:, :, HIST:EXT], 1.0 / w, rows[:, :, HIST:EXT],
                                         ALU.mult, ALU.subtract).then_inc(pooled, 1)

            for j in range(4):
                g = 12 + j
                for u in range(8):
                    split_lo(dve, 2 * g, u + LEAD)
                    if u == 3 and j:
                        pool(j - 1)
                for mt in range(2):
                    ext_row(2 * j + mt, mt, g)
            pool(3)
            for j in range(4):
                split_lo(dve, Q_POOL, j + LEAD)
                dve.wait_ge(d_hi, j + 1)
                if j == 0:
                    dve.wait_ge(new_done, 1)
                f = 2 * (j % 2)
                rows = ext[:, 2 * j:2 * j + 2]
                dve.tensor_tensor(f_lo[:, f:f + 2, 0:SEQ], rows[:, :, HIST:HIST + SEQ],
                                  f_hi[:, f:f + 2, 0:SEQ].bitcast(F32), ALU.subtract)
                for t in range(2):
                    i = dve.tensor_tensor(samples(f_lo[:, f + t]), ext_s(rows[:, t]),
                                          samples(f_hi[:, f + t]).bitcast(F32), ALU.subtract)
                i.then_inc(d_ready, 1)
                if j == 0:
                    for h in range(NH):
                        dve.wait_ge(act_hi_done, KT + h + 1)
                        dve.tensor_tensor(act_lo[:, h], qT[:, h], act_hi[:, h].bitcast(F32), ALU.subtract)\
                            .then_inc(act_ready, 1)
                for mt in range(2):
                    t = NH + 2 * j + mt
                    dve.wait_ge(act_hi_done, KT + t + 1)
                    i = dve.scalar_tensor_tensor(two(act_lo[:, t]), bank(mt), pscale[:, 2 * j + mt:2 * j + mt + 1],
                                                 two(act_hi[:, t]).bitcast(F32), ALU.mult, ALU.subtract)
                    i.then_inc(act_ready, 1)
                    dve.drain().then_inc(acc_free, 1)

            dve.memset(sq_sum, 0.0)
            with dve.Fori(0, 8) as g:
                for u in range(8):
                    split_lo(dve, 2 * g + Q_OUT, u + LEAD)
                for mt in range(2):
                    tile_done(dve, g + G_OUT, mt, 2 * g + Q_OUT, 7)
                    dve.tensor_copy(two(tile_of(acc, 2 * g + mt)), bank(mt)).then_inc(acc_free, 1)
                    dve.drain().then_inc(mix_out, 1)
                for mt in range(2):
                    dve.drain()
                    dve.wait_ge(sq_done, 2 * g + KT + mt + 1)
                    dve.tensor_tensor(sq_sum, sq_sum, sq[:, mt], ALU.add).then_inc(sq_added, 1)
            root_mean(2)

            def resid(kt):
                if kt == 0:
                    dve.wait_ge(x_again, 64)
                dve.wait_ge(scaled, kt + 1)
                dve.scalar_tensor_tensor(x2[:, kt], acc[:, kt], g_post[:, kt:kt + 1], x2[:, kt], ALU.mult, ALU.add)\
                    .then_inc(x2_ready, 1)

            def prep2(kt):
                if kt + 1 < KT:
                    resid(kt + 1)
                prep(kt, x2, g_fpre, 2 * KT)
                add_square(2 * KT + kt + 1, kt % 2, start=kt == 0)

            resid(0)
            prep2(0)
            prep2(1)

            def gate_group(c, j, odd, prepare=False):
                q, g, F = 2 * j + c * Q_CH + Q_FF + 2 * odd, j + c * G_CH + G_FF + odd, c * CH + j + odd
                pg, pu = banks(0, odd), banks(1, odd)
                for u in range(8):
                    split_lo(dve, q, u + LEAD)
                    if prepare and u < 7:
                        prep2(2 * u + 2)
                        prep2(2 * u + 3)
                if prepare:
                    root_mean(3)

                def p_(i):
                    return tile_of(par, F)[:, i:i + 1]
                dve.wait_ge(g_hist, F + 1)
                tile_done(dve, g, 0, q, 7)
                dve.tensor_tensor(g_ext[:, 2:2 + HN], pg[:, 0, 0:HN], rstd[:, 0:HN], ALU.mult)
                dve.tensor_tensor(g_ext[:, 2 + HN:2 + SEQ], pg[:, 1, 0:SEQ - HN], rstd[:, HN:SEQ], ALU.mult)
                dve.tensor_tensor(g_ext[:, 2 + SEQ:CEXT].rearrange("p (b n) -> p b n", b=DB)[:, :, 2:CSEG],
                                  pg[:, 1, SEQ - HN:HN].rearrange("p (b l) -> p b l", b=DB), samples(rstd),
                                  ALU.mult).then_inc(acc_free, 1)
                dve.drain().then_inc(g_ready, 1)
                tile_done(dve, g, 1, q, 7)
                dve.tensor_tensor(two(f_buf), pu[:, :, 0:HN], two(rstd[:, :]), ALU.mult).then_inc(acc_free, 1)
                dve.wait_ge(c_started, F + 1)
                dve.scalar_tensor_tensor(conv[:, 2:CEXT], g_ext[:, 1:CEXT - 1], p_(1), conv[:, 2:CEXT],
                                         ALU.mult, ALU.add)
                dve.drain()
                dve.scalar_tensor_tensor(conv[:, 2:CEXT], g_ext[:, 0:CEXT - 2], p_(0), conv[:, 2:CEXT],
                                         ALU.mult, ALU.add).then_inc(c_ready, 1)
                dve.wait_ge(gelu_done, F + 1)
                dve.tensor_tensor(f_buf[:, 0:SEQ], f_buf[:, 0:SEQ], conv[:, 2:2 + SEQ], ALU.mult)
                dve.tensor_tensor(samples(f_buf), samples(f_buf),
                                  conv[:, 2 + SEQ:CEXT].rearrange("p (b n) -> p b n", b=DB)[:, :, 2:CSEG],
                                  ALU.mult).then_inc(f_ready, 1)
                dve.wait_ge(f_hi_done, F + 1)
                dve.tensor_tensor(tile_of(f_lo, j + odd), f_buf, tile_of(f_hi, j + odd).bitcast(F32), ALU.subtract)\
                    .then_inc(f_split, 1)

            def chunk(c, first=False, last=False):
                q0, g0 = c * Q_CH + Q_FF, c * G_CH + G_FF
                if first:
                    gate_group(c, 0, 0, prepare=True)
                    gate_group(c, 0, 1)
                with dve.Fori(1 if first else 0, CH // 2) as j:
                    for odd in range(2):
                        gate_group(c, 2 * j, odd)

                def down(d, ahead):
                    for k in range(4):
                        if k < ahead:
                            split_lo(dve, d + q0 + 2 * CH, k + LEAD)
                        if k >= 2:
                            for mt in range(2):
                                i, g = k - 2, 2 * d + g0 + CH + k - 2
                                t = tile_of(acc, 4 * d + 2 * i + mt)
                                tile_done(dve, g, mt, d + q0 + 2 * CH, k)
                                if first:
                                    o = dve.tensor_copy(two(t), bank(mt, i))
                                else:
                                    o = dve.tensor_tensor(two(t), two(t), bank(mt, i), ALU.add)
                                o.then_inc(acc_free, 1)
                                if last:
                                    dve.drain().then_inc(mix_out, 1)
                    if last:
                        for i in range(4):
                            m = 4 * d + i
                            dve.drain()
                            dve.wait_ge(sq_done, m + 3 * KT + 1)
                            dve.tensor_tensor(sq_sum, sq_sum, sq[:, i % 2], ALU.add).then_inc(sq_added, 1)
                if last:
                    dve.memset(sq_sum, 0.0)
                with dve.Fori(0, 3 if last else 4) as d:
                    down(d, 4)
                if last:
                    down(3, 1)

            chunk(0, first=True)
            with dve.Fori(1, NCH - 1) as c:
                chunk(c)
            chunk(NCH - 1, last=True)
            root_mean(4)
            for kt in range(KT):
                dve.wait_ge(scaled, KT + kt + 1)
                dve.scalar_tensor_tensor(x2[:, kt], acc[:, kt], g_fpost[:, kt:kt + 1], x2[:, kt], ALU.mult, ALU.add)\
                    .then_inc(y_ready, 1)

        @block.gpsimd
        def _(pool):
            def tile_of(t, m):
                return t[:, m] if isinstance(m, int) else t[:, bass.ds(m, 1)].rearrange("p a n -> p (a n)")

            def row(t, i):
                return t[i] if isinstance(i, int) else t[bass.ds(i, 1)].rearrange("a p n -> p (a n)")

            pool.memset(q_blk[:, :], 0.0).then_inc(q_zeroed, 1)
            with pool.Fori(4, 8) as g:
                for mt in range(2):
                    pool.wait_ge(st_ready, 2 * g + mt + 1)
                    pool.dma_start(row(kT_out, 2 * g - 8 + mt), stage[:, mt]).then_inc(st_stored[mt], 16)
                for mt in range(2):
                    pool.wait_ge(st_stored[mt], (g - 3) * 16)
                pool.sem_inc(st_free, 2)
            with pool.Fori(8, 12) as g:
                for mt in range(2):
                    pool.wait_ge(st_ready, 2 * g + mt + 1)
                    pool.dma_start(row(vT_out, 2 * g - 16 + mt), stage[:, mt]).then_inc(st_stored[mt], 16)
                for mt in range(2):
                    pool.wait_ge(st_stored[mt], (g - 3) * 16)
                pool.sem_inc(st_free, 2)
            pool.wait_ge(pa_stored, NH)
            pool.memset(ext[:, :, 0:HIST], 0.0)
            pool.dma_start(hist_in, pool_hist).then_inc(hist_loaded, 16)
            pool.wait_ge(hist_loaded, 16)
            h4 = hist_in.rearrange("p (t b n) -> p t b n", t=NH, b=DB)
            for t in range(NH):
                pool.tensor_copy(ext[:, t, HIST + SEQ:EXT].rearrange("p (b n) -> p b n", b=DB)[:, :, 0:HIST], h4[:, t])
            pool.drain().then_inc(hist_placed, 1)
            for t in range(NH):
                pool.wait_ge(ext_ready, t + 1)
                pool.dma_start(ext_out[t], ext[:, t]).then_inc(ext_stored, 16)

            def scale(n):
                pool.wait_ge(rstd_ready, n)
                for kt in range(KT):
                    pool.tensor_tensor(acc[:, kt], acc[:, kt], rstd[:, :], ALU.mult).then_inc(scaled, 1)

            scale(2)
            pool.wait_ge(par_loaded, 16)
            pool.wait_ge(rstd_ready, 3)

            def conv_rows(F):
                seg = g_ext[:, 2 + SEQ:CEXT].rearrange("p (b n) -> p b n", b=DB)
                pool.tensor_copy(seg[:, :, 0:2], tile_of(par, F)[:, 4:NPAR].rearrange("p (b n) -> p b n", b=DB))\
                    .then_inc(g_hist, 1)
                pool.wait_ge(g_ready, F + 1)
                t = tile_of(tails, F)
                pool.tensor_copy(t[:, 0:2], g_ext[:, SEQ:SEQ + 2])
                pool.tensor_copy(t[:, 2:TAIL].rearrange("p (b n) -> p b n", b=DB), seg[:, :, DL:CSEG])
                pool.drain()
                pool.wait_ge(c_ready, F + 1)

            with pool.Fori(0, FT) as F:
                pool.memset(g_ext[:, 0:2], 0.0)
                conv_rows(F)
            pool.drain().then_inc(tails_out, 1)
            pool.dma_start(tail_out, tails).then_inc(out_done, 16)
            scale(4)
            for i in range(4):
                pool.wait_ge(y_ready, 4 * i + 4)
                pool.dma_start(yT[:, 4 * i:4 * i + 4], x2[:, 4 * i:4 * i + 4]).then_inc(out_done, 16)
            pool.wait_ge(out_done, 80)
            pool.wait_ge(ext_stored, 16 * NH)
            for mt in range(2):
                pool.wait_ge(st_stored[mt], 16 * 8)


def _layout(a):
    import numpy as np

    def cols(w, nk, width=256):
        k, n = w.shape
        return w.reshape(k // 256, 2, P, n // width, width).transpose(3, 0, 2, 1, 4)

    def vec(v):
        return v.reshape(-1, P).T

    xT = np.concatenate([a["x_prompt"].reshape(SEQ, D), a["x_sample"].reshape(NS, D)]).T
    xT = np.ascontiguousarray(xT.reshape(KT, P, NT).transpose(1, 0, 2))
    w_in, half = a["w_in"][0], D // 2
    order = [3, 2, 1, 0]
    u = w_in[:, 0:half].reshape(D, 4, 256)[:, order].reshape(D, half)
    w_in = np.concatenate([w_in[:, half:], u], axis=1)
    w_out = a["w_out"][0]
    w_out = np.concatenate([w_out[half:], w_out[0:half].reshape(4, 256, D)[order].reshape(half, D)])
    wp = a["w_pool"][0][order]
    parts = [cols(w_in, 0).reshape(-1, P, 512), np.concatenate([cols(wp[j], 0).reshape(-1, P, 512) for j in range(4)]),
             cols(w_out, 0).reshape(-1, P, 512)]
    gate_up = np.stack([a["w_gate"][0].reshape(D, FT, P), a["w_up"][0].reshape(D, FT, P)], 2).reshape(D, FT * 256)
    gu = cols(gate_up, 0).reshape(NCH, CH * 8, P, 512)
    dn = a["w_down"][0].reshape(NCH, CH * P, D)
    dn = np.stack([cols(dn[c], 0).reshape(4, 2, 2, P, 512).transpose(0, 2, 1, 3, 4).reshape(16, P, 512)
                   for c in range(NCH)])
    parts.append(np.concatenate([gu, dn], axis=1).reshape(-1, P, 512))
    units = np.concatenate(parts)
    assert units.shape[0] == UNITS
    kc = np.ascontiguousarray(a["cache_k"][0].transpose(0, 3, 1, 2)).reshape(N_PHYS, P, NH * PAGE)
    vc = np.ascontiguousarray(a["cache_v"][0].transpose(0, 2, 1, 3)).reshape(N_PHYS, PAGE, NH * P)
    ps = a["pool_scale"][0].reshape(4, 256)[order].reshape(-1)
    gains = np.concatenate([vec(a[n][0]) for n in ("g_mix_pre", "g_mix_post", "g_ffn_pre", "g_ffn_post")]
                           + [vec(ps)], axis=1)
    ph = a["state_pool"][0].reshape(DB, HIST, 4, 256)[:, :, order].reshape(DB, HIST, NH, P)
    pool_hist = np.ascontiguousarray(ph.transpose(3, 2, 0, 1)).reshape(P, NH * DB * HIST)
    cw = a["conv_w"][0].reshape(3, FT, P).transpose(2, 1, 0)
    cb = a["conv_b"][0].reshape(FT, P).T[:, :, None]
    ch = a["state_conv"][0].reshape(DB, 2, FT, P).transpose(3, 2, 0, 1).reshape(P, FT, 2 * DB)
    conv_par = np.concatenate([cw, cb, ch], axis=2)
    pos = np.concatenate([np.arange(SEQ), np.tile(PAGES * PAGE + np.arange(DL), DB)]).astype(np.float32)
    inv = np.float32(500000.0) ** (-np.arange(16, dtype=np.float32) * np.float32(2.0 / 32))
    ang = (inv[:, None].astype(np.float32) * pos[None, :]).astype(np.float32)
    c, s = np.cos(ang).astype(np.float32), np.sin(ang).astype(np.float32)
    rope_tab = np.stack([np.concatenate([c, c]), np.concatenate([-s, s])], axis=1)
    cst = np.zeros((P, 544), np.float32)
    cst[:, 0:128] = np.eye(P)
    cst[:, 128:256] = 1.0
    i = np.arange(P)
    cst[:, 256:384] = np.where(i[None, :] <= i[:, None], 0.0, NEG)
    j = np.arange(HC)
    same = (j[:, None] // DL == j[None, :] // DL) & (j[None, :] % DL <= j[:, None] % DL)
    cst[0:NS, 384:416] = np.where(same, 0.0, NEG)
    b = np.arange(NBLK)
    cst[0:NS, 416:480] = (b[None, :] < b[:, None]).astype(np.float32).reshape(1, 64)
    t = np.arange(16)
    cst[:, 480:544] = np.concatenate([w / np.minimum(t + 1, w) for w in WINDOWS])[None, :]
    table = np.ascontiguousarray(a["page_table"]).reshape(DB * 2, PAGES // 2)
    return {"xT": xT, "units": units, "kcache": kc, "vcache": vc, "table": table, "gains": gains,
            "pool_hist": pool_hist, "conv_par": conv_par, "rope_tab": rope_tab, "consts": cst}


_OUTS = {"yT": (P, KT, NT), "kT_out": (NH, P, NT), "vT_out": (NH, P, NT), "ext_out": (NH, P, EXT),
         "tail_out": (P, FT, TAIL)}


def kernel(**inputs):
    import numpy as np
    import concourse.bacc as bacc
    from concourse.bass_utils import run_bass_kernel_spmd

    a = {k: np.asarray(v) for k, v in inputs.items()}
    arrays = {k: np.ascontiguousarray(v) for k, v in _layout(a).items()}
    nc = bacc.Bacc("TRN2", target_bir_lowering=False, num_devices=1)
    aps = {k: nc.dram_tensor(k, v.shape, mybir.dt.from_np(v.dtype), kind="ExternalInput").ap()
           for k, v in arrays.items()}
    aps |= {k: nc.dram_tensor(k, s, F32, kind="ExternalOutput").ap() for k, s in _OUTS.items()}
    build(nc, **aps)
    r = run_bass_kernel_spmd(nc, [arrays], core_ids=[0]).results[0]
    y = r["yT"].transpose(2, 1, 0).reshape(NT, D)

    def heads(t):
        t = t.transpose(0, 2, 1)
        dec = t[:, SEQ:].reshape(NH, DB, DL, P).transpose(1, 0, 2, 3)
        return t[None, None, :, 0:SEQ], dec[None]

    kp, ks = heads(r["kT_out"])
    vp, vs = heads(r["vT_out"])
    e = r["ext_out"].reshape(4, 2, P, EXT)[[3, 2, 1, 0]].reshape(NH * P, EXT)
    pp = e[:, SEQ:SEQ + HIST].T
    pd = e[:, HIST + SEQ:].reshape(NH * P, DB, SEG)[:, :, DL:].transpose(1, 2, 0)
    t = r["tail_out"].transpose(2, 1, 0).reshape(TAIL, FF)
    out = (y[0:SEQ][None], y[SEQ:].reshape(DB, DL, D), kp, vp, ks, vs, pp[None, None], pd[None],
           t[0:2][None, None], t[2:].reshape(1, DB, 2, FF))
    return tuple(np.ascontiguousarray(o) for o in out)
```

```python
from contextlib import ExitStack

import concourse.bass as bass
from concourse import mybir

F32 = mybir.dt.float32
F32R = mybir.dt.float32r
I32 = mybir.dt.int32
ALU = mybir.AluOpType
ACT = mybir.ActivationFunctionType
AX = mybir.AxisListType

P = 128
D = 2048
KT = D // P
SEQ = 512
DB, DL = 8, 4
NS = DB * DL
NT = SEQ + NS
HN = NT // 2
NH = 8
PAGES = 16
PAGE = 128
N_PHYS = 160
NBLK = PAGES // 2
TOPK = 3
HC = NH * DL
FF = 5632
FT = FF // P
CH = 4
NCH = FT // CH
HIST = 15
SEG = HIST + DL
EXT = HIST + SEQ + DB * SEG
WINDOWS = (16, 8, 4, 2)
CSEG = 2 + DL
CEXT = 2 + SEQ + DB * CSEG
TAIL = 2 + 2 * DB
NPAR = 4 + 2 * DB
SCALE = float(P) ** -0.5
NEG = -1.0e30
EPS = 1.0e-6
RING = 4
LEAD = 3
G_POOL = 16
G_OUT = G_POOL + 4
G_FF = G_OUT + 8
G_CH = CH + 8
Q_POOL = 32
Q_OUT = Q_POOL + 1
Q_FF = Q_OUT + 16
Y_POOL = (1, 3, 5, 7, 9, 11, 13)
K_POOL = (0, 1, 6, 7)
K_OUT = (2, 3, 4, 5, 8, 9, 10, 11)
Q_CH = 2 * CH + 4
UNITS = 4 * (Q_FF + NCH * Q_CH)


def build(nc, xT, units, kcache, vcache, table, gains, pool_hist, conv_par, rope_tab, consts,
          yT, kT_out, vT_out, ext_out, tail_out):
    with ExitStack() as ctx:
        def sb(name, shape, dt=F32):
            return ctx.enter_context(nc.sbuf_tensor(name, shape, dt))

        def sem(name):
            return ctx.enter_context(nc.semaphore(name))

        act_hi = sb("act_hi", [P, KT, NT], F32R)
        act_lo = sb("act_lo", [P, KT, NT], F32R)
        w_raw = sb("w_raw", [P, RING, 2, 256])
        w_hi = sb("w_hi", [P, RING, 2, 256], F32R)
        w_lo = sb("w_lo", [P, RING, 2, 256], F32R)
        R1 = NH * NT + NH * EXT
        reg1 = sb("region1", [P, R1])
        x_in = reg1[:, 0:KT * NT].rearrange("p (k n) -> p k n", k=KT)
        qT = reg1[:, 0:NH * NT].rearrange("p (h n) -> p h n", h=NH)
        kT = reg1[:, NH * NT:2 * NH * NT].rearrange("p (h n) -> p h n", h=NH)
        ext = reg1[:, NH * NT:R1].rearrange("p (t n) -> p t n", t=NH)
        prob = reg1[:, 2 * NH * NT:2 * NH * NT + 1024].rearrange("p (s n) -> p s n", s=2)
        acc = reg1[:, 0:KT * NT].rearrange("p (k n) -> p k n", k=KT)
        par = reg1[:, KT * NT:KT * NT + FT * NPAR].rearrange("p (t n) -> p t n", t=FT)
        R2 = 3 * 4096 + NH * P
        base2 = nc.sbuf_base
        reg2 = sb("region2", [P, R2])
        assert nc.sbuf_base - base2 == 4 * R2
        v_tok = reg2[:, 0:4096].rearrange("p (h t d) -> p h t d", h=NH, t=4)
        s_all = reg2[:, 4096:8192].rearrange("p (b n) -> p b n", b=DB)
        pages = reg2[:, 8192:12288].rearrange("p (s n) -> p s n", s=RING)
        v_new = reg2[0:HC, 12288:R2].rearrange("p (b d) -> p b d", b=DB)
        o_all = reg2[:, 0:8192].rearrange("p (a n) -> p a n", a=2)[:, :, 0:NH * P]
        hist_in = reg2[:, 0:NH * DB * HIST]
        win = reg2[:, 1024:1024 + 4 * EXT].rearrange("p (s t n) -> p s t n", s=2, t=2)
        x2 = reg2[:, 0:KT * NT].rearrange("p (k n) -> p k n", k=KT)
        f_hi = nc.alloc_sbuf_tensor_at("f_hi", [P, CH, NT], F32R, offset=base2 + 4 * KT * NT)
        f_lo = nc.alloc_sbuf_tensor_at("f_lo", [P, CH, NT], F32R, offset=base2 + 4 * (KT + CH) * NT)
        assert (KT + 2 * CH) * NT <= R2 and FT * NPAR <= R1 - KT * NT
        scratch = sb("scratch", [P, 4, CEXT])
        stage = scratch[:, 0:2, 0:NT]
        sq = scratch[:, 0:2, 0:NT]
        probT = scratch[:, :, :].rearrange("p a n -> p (a n)")[:, 0:4 * SEQ].rearrange("p (k n) -> p k n", k=4)
        swap = scratch[0:32, 2, 0:NT]
        sq_sum = scratch[:, 3, 0:NT]
        tmp = scratch[:, 2, 0:NT]
        g_ext, conv, f_buf = scratch[:, 0, :], scratch[:, 1, :], scratch[:, 2, 0:NT]
        rstd = sb("rstd", [P, NT])
        shared = sb("shared", [P, 2, NT])
        cos_t, sin_t = shared[0:32, 0, :], shared[0:32, 1, :]
        p_seq = shared[:, :, 0:PAGES * HC]
        tails = shared[:, :, :].rearrange("p a n -> p (a n)")[:, 0:FT * TAIL].rearrange("p (t n) -> p t n", t=FT)
        cst = sb("cst", [P, 128 + 128 + 128 + 32 + 64 + 64])
        ident, ones, causal = cst[:, 0:128], cst[:, 128:256], cst[:, 256:384]
        new_mask = cst[0:NS, 384:416]
        below = cst[0:NS, 416:480].rearrange("p (i j) -> p i j", i=NBLK)
        corr = cst[:, 480:544].rearrange("p (w n) -> p w n", w=4)
        gain = sb("gain", [P, 4 * KT + NH])
        g_pre, g_post, g_fpre, g_fpost = (gain[:, i * KT:(i + 1) * KT] for i in range(4))
        pscale = gain[:, 4 * KT:]
        q_blk = sb("q_blk", [P, NH * (HC + DL)])
        p_new = sb("p_new", [HC, DB, HC])
        q_dec = sb("q_dec", [P, DB, HC])
        p_newT = q_dec[0:HC]
        v_dec = sb("v_dec", [P, DB, HC])
        gate = sb("gate", [HC, DB, NBLK])
        bmax = sb("bmax", [HC, DB, NBLK])
        rank = sb("rank", [HC, DB, NBLK])
        mx = sb("mx", [HC, 4, DB])
        bias4 = sb("bias4", [P, DB, 2])
        esum = sb("esum", [P, DB, 2])
        tot = sb("tot", [HC, DB, NBLK + 1])
        rinv = sb("rinv", [HC, DB])
        col = sb("col", [P, 16])

        ps = ctx.enter_context(nc.psum_tensor("ps_acc", [P, 2, 2, 512], F32))
        ps_a = ctx.enter_context(nc.psum_tensor("ps_a", [P, 2, 512], F32))
        ps_b = ctx.enter_context(nc.psum_tensor("ps_b", [P, 2, 512], F32))

        w_loaded = [sem(f"w_loaded{i}") for i in range(RING)]
        hi_ready = sem("hi_ready")
        lo_ready = sem("lo_ready")
        unit_used = sem("unit_used")
        acc_done = sem("acc_done")
        acc_free = sem("acc_free")
        act_ready = sem("act_ready")
        act_hi_done = sem("act_hi_done")
        sq_done = sem("sq_done")
        sq_added = sem("sq_added")
        ss_done = sem("ss_done")
        var_ready = sem("var_ready")
        root_done = sem("root_done")
        const_in = sem("const_in")
        x_loaded = [sem(f"x_loaded{i}") for i in range(4)]
        st_ready = sem("st_ready")
        st_copied = sem("st_copied")
        st_stored = [sem(f"st_stored{i}") for i in range(2)]
        st_free = sem("st_free")
        page_loaded = [sem(f"page_loaded{i}") for i in range(RING)]
        page_used = sem("page_used")
        q_zeroed = sem("q_zeroed")
        q_ready = sem("q_ready")
        scores_out = sem("scores_out")
        vt_done = sem("vt_done")
        vt_out = sem("vt_out")
        pe_s = sem("pe_s")
        dve_s = sem("dve_s")
        act_s = sem("act_s")
        pa_scores = sem("pa_scores")
        pa_max = sem("pa_max")
        pa_exp = sem("pa_exp")
        pa_norm = sem("pa_norm")
        pa_trans = sem("pa_trans")
        pa_copied = sem("pa_copied")
        pa_out = sem("pa_out")
        pa_stored = sem("pa_stored")
        pt_done = sem("pt_done")
        pt_out = sem("pt_out")
        new_out = sem("new_out")
        p_ready = sem("p_ready")
        pv_out = sem("pv_out")
        new_done = sem("new_done")
        ext_ready = sem("ext_ready")
        ext_stored = sem("ext_stored")
        hist_loaded = sem("hist_loaded")
        hist_placed = sem("hist_placed")
        pooled = sem("pooled")
        d_hi = sem("d_hi")
        d_ready = sem("d_ready")
        attn_ready = sem("attn_ready")
        mix_out = sem("mix_out")
        x_again = sem("x_again")
        par_loaded = sem("par_loaded")
        scaled = sem("scaled")
        x2_ready = sem("x2_ready")
        g_ready = sem("g_ready")
        g_hist = sem("g_hist")
        c_started = sem("c_started")
        c_ready = sem("c_ready")
        gelu_done = sem("gelu_done")
        f_ready = sem("f_ready")
        f_hi_done = sem("f_hi_done")
        f_split = sem("f_split")
        tails_out = sem("tails_out")
        rstd_ready = sem("rstd_ready")
        y_ready = sem("y_ready")
        y_pool = sem("y_pool")
        y_stored = sem("y_stored")
        out_done = sem("out_done")

        block = ctx.enter_context(nc.Block())

        def load_unit(sp, q, k, first=False):
            if not first:
                sp.wait_ge(lo_ready, 4 * q + k - RING + 1)
            u = 4 * q + k
            src = units[u] if isinstance(u, int) else units[bass.ds(u, 1)].rearrange("a p n -> p (a n)")
            sp.dma_start(w_raw[:, k % RING].rearrange("p a n -> p (a n)"), src).then_inc(w_loaded[k % RING], 16)

        def split_hi(act, q, k, first=False):
            s = k % RING
            act.wait_ge(w_loaded[s], 16 * (q + k // RING + 1))
            if not first:
                act.wait_ge(unit_used, 4 * q + k - RING + 1)
            act.activation(w_hi[:, s], w_raw[:, s], ACT.Copy).then_inc(hi_ready, 1)

        def split_lo(dve, q, k):
            s = k % RING
            dve.wait_ge(hi_ready, 4 * q + k + 1)
            dve.tensor_tensor(w_lo[:, s], w_raw[:, s], w_hi[:, s].bitcast(F32), ALU.subtract).then_inc(lo_ready, 1)

        def tile_done(eng, G, mt, q, k):
            if mt == 0:
                eng.wait_ge(acc_done, G + 1)
            else:
                eng.wait_ge(unit_used, 4 * q + k + 1)

        def half(ap, i):
            return ap[:, i * HN:(i + 1) * HN]

        def banks(mt, odd=0):
            return (ps_a, ps_b)[mt] if odd else ps[:, mt]

        def bank(mt, odd=0):
            return banks(mt, odd)[:, :, 0:HN]

        def two(ap):
            return ap.rearrange("p (a n) -> p a n", a=2)

        @block.sync
        def _(sp):
            pg = [sp.alloc_register(f"page{i}") for i in range(8)]

            def load_x(i):
                sp.dma_start(x_in[:, 4 * i:4 * i + 4], xT[:, 4 * i:4 * i + 4]).then_inc(x_loaded[i], 16)

            def load_page(cache, slot, reg, used):
                if used is not None:
                    sp.wait_ge(page_used, used)
                i = sp.snap(reg, min_val=0, max_val=N_PHYS - 1)
                sp.dma_start(pages[:, slot], cache[bass.ds(i, 1)].rearrange("a p n -> p (a n)"))\
                    .then_inc(page_loaded[slot], 16)

            sp.dma_start(gain[:], gains).then_inc(const_in, 16)
            load_x(0)
            load_unit(sp, 0, 0, first=True)
            load_unit(sp, 0, 1, first=True)
            load_x(1)
            load_unit(sp, 0, 2, first=True)
            load_x(2)
            load_unit(sp, 0, 3, first=True)
            load_x(3)
            sp.dma_start(cst[:], consts).then_inc(const_in, 16)
            sp.dma_start(shared[0:32], rope_tab).then_inc(const_in, 16)
            with sp.Fori(0, 4) as g:
                for u in range(8):
                    load_unit(sp, 2 * g, u + RING)
            with sp.Fori(4, 12) as g:
                for u in range(8):
                    if u % 4 == 0:
                        sp.load(pg, table[bass.ds(2 * g - 8 + u // 4, 1), :])
                    load_unit(sp, 2 * g, u + RING)
                    for i in (2 * u, 2 * u + 1):
                        load_page(kcache, i % RING, pg[i % 8], 16 * g - 64 + i + 1)
            with sp.Fori(12, 16) as g:
                for u in range(8):
                    if u % 2 == 0:
                        sp.load(pg, table[bass.ds(4 * g - 48 + u // 2, 1), :])
                    load_unit(sp, 2 * g, u + RING)
                    for i in range(4 * u, 4 * u + 4):
                        load_page(vcache, i % RING, pg[i % 8], 32 * g - 384 + 128 + i + 1)
            for k in range(12):
                load_unit(sp, Q_POOL, k + RING)
            sp.wait_ge(act_ready, 2 * KT)
            sp.wait_ge(new_done, 1)
            for i in range(4):
                sp.dma_start(x2[:, 4 * i:4 * i + 4], xT[:, 4 * i:4 * i + 4]).then_inc(x_again, 16)
            sp.dma_start(par, conv_par).then_inc(par_loaded, 16)
            with sp.Fori(1, 8) as g:
                for u in range(8):
                    load_unit(sp, 2 * g + Q_OUT, u + RING)
            with sp.Fori(0, NCH - 1) as c:
                for k in range(4 * Q_CH):
                    load_unit(sp, c * Q_CH + Q_FF, k + RING)
            for k in range(4 * Q_CH - RING):
                load_unit(sp, (NCH - 1) * Q_CH + Q_FF, k + RING)
            for i in range(KT // 2):
                by_pool = sum(kt in Y_POOL for kt in range(2 * i + 2))
                sp.wait_ge(y_ready, 2 * i + 2 - by_pool)
                sp.wait_ge(y_pool, by_pool)
                sp.dma_start(yT[:, 2 * i:2 * i + 2], x2[:, 2 * i:2 * i + 2]).then_inc(y_stored, 16)
            sp.wait_ge(y_stored, 16 * KT // 2)

        @block.scalar
        def _(act):
            def act_tile(kt, src, g, hi=None):
                act.activation(act_hi[:, kt], src, ACT.Copy, scale=g[:, kt:kt + 1]).then_inc(act_hi_done, 1)

            def squares(src, s, freed):
                if freed is not None:
                    act.wait_ge(sq_added, freed)
                act.activation(sq[:, s], src, ACT.Square).then_inc(sq_done, 1)

            def root(n):
                act.wait_ge(var_ready, n)
                act.activation(rstd[:, :], tmp, ACT.Sqrt).then_inc(root_done, 1)

            act.sem_inc(scores_out, 2)
            act.sem_inc(vt_out, 2)
            act.sem_inc(pv_out, 2)
            act.sem_inc(st_free, 2)

            def prep(kt):
                if kt == 0:
                    act.wait_ge(const_in, 16)
                if kt % 4 == 0:
                    act.wait_ge(x_loaded[kt // 4], 16)
                act_tile(kt, x_in[:, kt], g_pre)
                squares(x_in[:, kt], kt % 2, kt - 1 if kt >= 2 else None)

            split_hi(act, 0, 0, first=True)
            prep(0)
            prep(1)
            split_hi(act, 0, 1, first=True)
            split_hi(act, 0, 2, first=True)
            for u in range(8):
                split_hi(act, 0, u + LEAD, first=u + LEAD < RING)
                if u < 7:
                    prep(2 * u + 2)
                    prep(2 * u + 3)
            split_hi(act, 2, LEAD)
            root(1)
            split_hi(act, 2, 1 + LEAD)
            split_hi(act, 2, 2 + LEAD)

            def copy_heads(dst, g0, g):
                for mt in range(2):
                    act.wait_ge(st_ready, 2 * g + mt + 1)
                    h = 2 * (g - g0) + mt
                    out = dst[:, h] if isinstance(h, int) else dst[:, bass.ds(h, 1)].rearrange("p a n -> p (a n)")
                    act.activation(out, stage[:, mt], ACT.Copy).then_inc(st_copied, 1)

            copy_heads(qT, 0, 0)
            for u in range(3, 8):
                split_hi(act, 2, u + LEAD)
            copy_heads(qT, 0, 1)
            with act.Fori(2, 4) as g:
                for u in range(8):
                    split_hi(act, 2 * g, u + LEAD)
                copy_heads(qT, 0, g)

            def load_q(b):
                act.wait_ge(page_used, 16 * b + RING)
                src = qT[:, :, bass.ds(b * DL + SEQ, DL)]
                act.activation(q_blk[:, :].rearrange("p (h l) -> p h l", h=NH)[:, :, 0:DL], src, ACT.Copy)\
                    .then_inc(q_ready, 1)

            def store_scores(b, quad):
                act.wait_ge(page_used, 16 * b + 4 * quad + 4 + RING)
                act.activation(s_all[quad * HC:(quad + 1) * HC, bass.ds(b, 1)].rearrange("p a n -> p (a n)"),
                               ps_a[0:HC, quad % 2, :], ACT.Copy).then_inc(scores_out, 1)

            def kv_group(g):
                load_q(g - 4)
                for u in range(8):
                    split_hi(act, 2 * g, u + LEAD)
                    if u in (3, 5, 7):
                        store_scores(g - 4, u // 2 - 1)

            with act.Fori(4, 8) as g:
                act.wait_ge(st_copied, 8)
                act.wait_ge(q_zeroed, 1)
                kv_group(g)
                store_scores(g - 4, 3)
                copy_heads(kT, 4, g)
            with act.Fori(8, 12) as g:
                kv_group(g)
                for mt in range(2):
                    act.wait_ge(st_ready, 2 * g + mt + 1)
                    act.activation(v_dec[:, :, bass.ds((2 * g - 16 + mt) * DL, DL)],
                                   stage[:, mt, SEQ:NT].rearrange("p (b l) -> p b l", b=DB), ACT.Copy)\
                        .then_inc(st_copied, 1)
                store_scores(g - 4, 3)
                for mt in range(2):
                    act.wait_ge(vt_done, 2 * g - 15 + mt)
                    act.activation(v_tok[:, bass.ds(2 * g - 16 + mt, 1)].rearrange("p a t d -> p (a t d)"),
                                   ps_b[:, mt, :], ACT.Copy).then_inc(vt_out, 1)

            act.activation(q_dec[:, :, :].rearrange("p b (h l) -> p h b l", h=NH),
                           qT[:, :, SEQ:NT].rearrange("p h (b l) -> p h b l", b=DB), ACT.Copy).then_inc(q_ready, 1)
            act.wait_ge(pe_s, 2)
            act.activation(v_new.rearrange("p (a b) d -> p a (b d)", a=2), ps[0:HC, 1], ACT.Copy).then_inc(new_out, 1)

            def decode_exp(b):
                if b == 0:
                    act.wait_ge(dve_s, 2)
                for k in range(2):
                    c = s_all[:, b, k * 256:(k + 1) * 256]
                    act.activation(c, c, ACT.Exp, scale=SCALE, bias=bias4[:, b, k:k + 1],
                                   accum_out=esum[:, b, k:k + 1])
                act.activation(p_new[:, b], p_new[:, b], ACT.Exp, scale=SCALE, bias=mx[:, 3, b:b + 1],
                               accum_out=tot[:, b, NBLK:NBLK + 1]).then_inc(act_s, 1)

            act.wait_ge(st_free, 2 * 8 + 2)

            def exps(t):
                n = (t % 4 + 1) * P
                act.wait_ge(pa_max, t + 1)
                if t >= 2:
                    act.wait_ge(pa_trans, t - 1)
                act.activation(prob[:, t % 2, 0:n], ps_a[:, t % 2, 0:n], ACT.Exp, scale=SCALE,
                               bias=col[:, t % 2:t % 2 + 1], accum_out=col[:, 2 + t % 2:3 + t % 2]).then_inc(pa_exp, 1)

            def prompt_store(h):
                act.wait_ge(pa_out, h + 1)
                act.activation(qT[:, h, 0:SEQ], ps[:, 0, h % 2, :], ACT.Copy).then_inc(pa_stored, 1)

            exps(0)
            for t in range(4 * NH):
                h, qi = divmod(t, 4)
                n = (qi + 1) * P
                if t + 1 < 4 * NH:
                    exps(t + 1)
                act.wait_ge(pa_trans, t + 1)
                if qi == 0 and h:
                    prompt_store(h - 1)
                act.activation(probT[:, 0:qi + 1, qi * P:(qi + 1) * P],
                               ps_b[:, t % 2, 0:n].rearrange("p (k n) -> p k n", k=qi + 1), ACT.Copy)\
                    .then_inc(pa_copied, 1)
                if qi == 1:
                    decode_exp(h)
            prompt_store(NH - 1)
            act.wait_ge(pe_s, 3)
            act.activation(p_newT.rearrange("p b n -> p (b n)"), ps_a[0:HC, 0, 0:DB * HC], ACT.Copy)\
                .then_inc(new_out, 1)

            act.wait_ge(pt_out, DB)
            act.wait_ge(dve_s, 3)

            def store_values(i, s):
                act.wait_ge(hist_placed, 1)
                act.wait_ge(page_used, 64 * i + 16 * s + 144 + RING)
                act.activation(o_all[s * HC:(s + 1) * HC, bass.ds(i, 1)].rearrange("p a n -> p (a n)"),
                               (ps_a, ps_b)[s % 2][0:HC, :, :].rearrange("p a n -> p (a n)"), ACT.Copy,
                               scale=rinv[:, bass.ds(4 * i + s, 1)]).then_inc(pv_out, 1)

            with act.Fori(0, 2) as i:
                for s in range(4):
                    act.wait_ge(page_used, 64 * i + 16 * s + 112 + RING)
                    act.activation(p_seq[:, s % 2], s_all[:, bass.ds(4 * i + s, 1)].rearrange("p a n -> p (a n)"),
                                   ACT.Copy).then_inc(p_ready, 1)
                    for u in range(4 * s, 4 * s + 4):
                        split_hi(act, 4 * i + 2 * 12, u + LEAD)
                    store_values(i, s)
            def pool_hi(j):
                act.wait_ge(pooled, j + 1)
                if j == 0:
                    act.wait_ge(page_used, 2 * DB * PAGES + RING)
                if j >= 2:
                    act.wait_ge(unit_used, 4 * Q_POOL + K_POOL[j - 2] + 1)
                f = 2 * (j % 2)
                act.activation(f_hi[:, f:f + 2, 0:SEQ], ext[:, 2 * j:2 * j + 2, HIST:HIST + SEQ], ACT.Copy)
                for t in range(2):
                    i = act.activation(f_hi[:, f + t, SEQ:NT].rearrange("p (b l) -> p b l", b=DB),
                                       ext_s(ext[:, 2 * j + t]), ACT.Copy)
                i.then_inc(d_hi, 1)

            def ext_s(row):
                return row[:, HIST + SEQ:EXT].rearrange("p (b n) -> p b n", b=DB)[:, :, HIST:SEG]

            def pooled_hi(j):
                for mt in range(2):
                    tile_done(act, G_POOL + j, mt, Q_POOL, K_POOL[j])
                    t = NH + 2 * j + mt
                    act.activation(two(act_hi[:, t]), bank(mt), ACT.Copy, scale=pscale[:, 2 * j + mt:2 * j + mt + 1])\
                        .then_inc(act_hi_done, 1)

            pool_hi(0)
            act.wait_ge(new_done, 1)
            act.activation(act_hi[:, 0:NH, SEQ:NT], ps_a[:, 0, 0:DB * HC].rearrange("p (h n) -> p h n", h=NH),
                           ACT.Copy).then_inc(act_hi_done, NH)
            pool_hi(1)
            for k in range(12):
                split_hi(act, Q_POOL, k + LEAD)
                if k in K_POOL:
                    pooled_hi(K_POOL.index(k))
                if k in (2, 3):
                    pool_hi(k)

            def mix_squares(g):
                for mt in range(2):
                    act.wait_ge(mix_out, 2 * g + mt + 1)
                    m = 2 * g + mt
                    act.wait_ge(sq_added, KT - 1 + m)
                    act.activation(sq[:, mt], tile_of(acc, m), ACT.Square).then_inc(sq_done, 1)

            def tile_of(t, m):
                return t[:, m] if isinstance(m, int) else t[:, bass.ds(m, 1)].rearrange("p a n -> p (a n)")

            mix_squares(0)
            with act.Fori(1, 8) as g:
                for u in range(8):
                    split_hi(act, 2 * g + Q_OUT, u + LEAD)
                mix_squares(g)
            root(2)

            def prep2(kt):
                act.wait_ge(x2_ready, kt + 1)
                act_tile(kt, x2[:, kt], g_fpre)
                squares(x2[:, kt], kt % 2, 2 * KT + kt - 1)

            def ff_gate(g, F):
                def p_(i):
                    if isinstance(F, int):
                        return par[:, F, i:i + 1]
                    return par[:, bass.ds(F, 1), i:i + 1].rearrange("p a n -> p (a n)")
                act.wait_ge(g_ready, F + 1)
                act.activation(conv[:, 2:CEXT], g_ext[:, 2:CEXT], ACT.Identity, scale=p_(2), bias=p_(3))\
                    .then_inc(c_started, 1)
                act.wait_ge(c_ready, F + 1)
                act.activation(conv[:, 2:CEXT], conv[:, 2:CEXT], ACT.Gelu_apprx_tanh).then_inc(gelu_done, 1)

            def f_part(F, j):
                act.wait_ge(f_ready, F + 1)
                act.activation(tile_of(f_hi, j), f_buf, ACT.Copy).then_inc(f_hi_done, 1)

            def chunk(c, first=False, last=False):
                q0 = c * Q_CH + Q_FF
                g0 = c * G_CH + G_FF

                def gate_group(j, prepare=False):
                    for u in range(8):
                        split_hi(act, 2 * j + q0, u + LEAD)
                        if prepare and u < 7:
                            prep2(2 * u + 2)
                            prep2(2 * u + 3)
                    if prepare:
                        root(3)
                    F = c * CH + j
                    ff_gate(j + g0, F)
                    f_part(F, j)
                if first:
                    prep2(0)
                    prep2(1)
                    gate_group(0, prepare=True)
                with act.Fori(1 if first else 0, CH) as j:
                    gate_group(j)
                with act.Fori(0, 3 if last else 4) as d:
                    for k in range(4):
                        split_hi(act, d + q0 + 2 * CH, k + LEAD)
                    if last:
                        for i in range(4):
                            last_squares(4 * d + i, i % 2)
                if last:
                    split_hi(act, q0 + 2 * CH + 3, LEAD)
                    for i in range(4):
                        last_squares(12 + i, i % 2)

            def last_squares(m, s):
                act.wait_ge(mix_out, m + KT + 1)
                act.wait_ge(tails_out, 1)
                act.wait_ge(sq_added, m + 3 * KT - 1)
                act.activation(sq[:, s], tile_of(acc, m), ACT.Square).then_inc(sq_done, 1)

            chunk(0, first=True)
            with act.Fori(1, NCH - 1) as c:
                chunk(c)
            chunk(NCH - 1, last=True)
            root(4)

        @block.tensor
        def _(pe):
            def group(G, q, nu, hi, lo, ready=None, after=None, k0=0, first=False, odd=0, units=None):
                for u in units or range(nu):
                    k = K_OUT[u] if units else k0 + u
                    pe.wait_ge(lo_ready, 4 * q + k + 1)
                    if ready is not None:
                        pe.wait_ge(*ready(u))
                    s = k % RING
                    for mt in range(2):
                        if u == 0 and not first:
                            pe.wait_ge(acc_free, 2 * G + mt - 1)
                        for i in range(2):
                            kt = 2 * u + i
                            cols = slice(mt * P, (mt + 1) * P)
                            for w, a in ((w_hi, hi), (w_hi, lo), (w_lo, hi)):
                                for n in range(2):
                                    mm = pe.matmul(banks(mt, odd)[:, n, 0:HN], w[:, s, i, cols], half(a[:, kt], n),
                                                   start=kt == 0 and w is w_hi and a is hi,
                                                   stop=kt == 2 * nu - 1 and w is w_lo)
                        if u == nu - 1 and mt == 0:
                            mm.then_inc(acc_done, 1)
                    mm.then_inc(unit_used, 1)
                    if after is not None:
                        after(u)

            def ff_unit(G, q, k, u, nu, hi, lo, odd, ready, prev=2):
                pe.wait_ge(lo_ready, 4 * q + k + 1)
                s = k % RING
                for i in range(2):
                    kt = 2 * u + i
                    if ready is not None:
                        pe.wait_ge(*ready(kt))
                    for mt in range(2):
                        if kt == 0:
                            pe.wait_ge(acc_free, 2 * G + mt + 1 - 2 * prev)
                        cols = slice(mt * P, (mt + 1) * P)
                        for w, a in ((w_hi, hi), (w_hi, lo), (w_lo, hi)):
                            for n in range(2):
                                mm = pe.matmul(banks(mt, odd)[:, n, 0:HN], w[:, s, i, cols], half(a[:, kt], n),
                                               start=kt == 0 and w is w_hi and a is hi,
                                               stop=kt == 2 * nu - 1 and w is w_lo)
                        if kt == 2 * nu - 1 and mt == 0:
                            mm.then_inc(acc_done, 1)
                mm.then_inc(unit_used, 1)

            def sum_squares(n):
                pe.wait_ge(sq_added, n)
                for i in range(2):
                    mm = pe.matmul(ps_a[:, i, 0:HN], ones, half(sq_sum, i), start=True, stop=True)
                mm.then_inc(ss_done, 1)

            def ready1(u):
                return act_ready, 2 * u + 2

            group(0, 0, 8, act_hi, act_lo, ready1, first=True)
            pe.wait_ge(const_in, 48)
            sum_squares(KT)
            pe.wait_ge(var_ready, 1)
            group(1, 2, 8, act_hi, act_lo, first=True, odd=1)
            with pe.Fori(2, 4) as g:
                group(g, 2 * g, 8, act_hi, act_lo)

            def scores(g):
                b = g - 4

                def pair(n):
                    quad, s = n // 2, 2 * (n % 2)
                    for i in range(2):
                        pe.wait_ge(page_loaded[s + i], (b * 4 + quad + 1) * 16)
                    if n == 0:
                        pe.wait_ge(q_ready, b + 1)
                    if s == 0:
                        pe.wait_ge(scores_out, 4 * b + quad + 1)
                    for h in range(NH):
                        mm = pe.matmul(ps_a[0:HC, quad % 2, s * P:(s + 2) * P], q_blk[:, h * HC:(h + 1) * HC],
                                       pages[:, s:s + 2, h * P:(h + 1) * P], start=h == 0, stop=h == NH - 1)
                    mm.then_inc(page_used, 2)

                def after(u):
                    if u:
                        pair(u - 1)
                    if u == 7:
                        pair(7)
                return after

            pe.sem_inc(page_used, RING)
            with pe.Fori(4, 8) as g:
                group(g, 2 * g, 8, act_hi, act_lo, after=scores(g))
            with pe.Fori(8, 12) as g:
                group(g, 2 * g, 8, act_hi, act_lo, after=scores(g))
                pe.wait_ge(vt_out, 2 * g - 16 + 2)
                for mt in range(2):
                    pe.wait_ge(st_ready, 2 * g + mt + 1)
                    for t in range(4):
                        mm = pe.transpose(ps_b[:, mt, t * P:(t + 1) * P], stage[:, mt, t * P:(t + 1) * P], ident)
                    mm.then_inc(vt_done, 1)

            pe.wait_ge(st_copied, 24)
            pe.wait_ge(q_ready, DB + 1)
            pe.wait_ge(acc_free, 24)
            for b in range(DB):
                new = slice(SEQ + b * DL, SEQ + (b + 1) * DL)
                mm = pe.matmul(ps[0:HC, 0, 0, b * HC:(b + 1) * HC], q_dec[:, b], kT[:, :, new],
                               start=True, stop=True)
            mm.then_inc(pe_s, 1)
            for b in range(DB):
                mm = pe.transpose(ps[0:HC, 1, b // 4, (b % 4) * P:(b % 4 + 1) * P], v_dec[:, b],
                                  ident)
            mm.then_inc(pe_s, 1)

            def prompt_scores(t):
                h, qi = divmod(t, 4)
                n = (qi + 1) * P
                if t >= 2:
                    pe.wait_ge(pa_exp, t - 1)
                q = qT[:, h, qi * P:(qi + 1) * P]
                if qi:
                    pe.matmul(ps_a[:, t % 2, 0:n - P], q, kT[:, h, 0:n - P], start=True, stop=True)
                pe.matmul(ps_a[:, t % 2, n - P:n], q, kT[:, h, n - P:n], start=True, stop=False)
                pe.matmul(ps_a[:, t % 2, n - P:n], ident, causal, start=False, stop=True).then_inc(pa_scores, 1)

            def decode_transposes(b):
                pe.wait_ge(act_s, b + 1)
                if b == 0:
                    pe.wait_ge(new_out, 1)
                if b >= 2:
                    pe.wait_ge(pt_out, b - 1)
                for c in range(4):
                    mm = pe.transpose(ps[:, 1, b % 2, c * P:(c + 1) * P], s_all[:, b, c * P:(c + 1) * P], ident)
                mm.then_inc(pt_done, 1)

            pe.wait_ge(scores_out, 4 * DB + 2)
            def prompt_values(h):
                pe.wait_ge(pa_copied, 4 * h + 4)
                if h == 0:
                    pe.wait_ge(dve_s, 1)
                if h >= 2:
                    pe.wait_ge(pa_stored, h - 1)
                for kj in range(4):
                    mm = pe.matmul(ps[:, 0, h % 2, kj * P:SEQ], v_tok[:, h, kj], probT[:, kj, kj * P:SEQ],
                                   start=kj == 0, stop=kj == 3)
                mm.then_inc(pa_out, 1)
                decode_transposes(h)

            prompt_scores(0)
            prompt_scores(1)
            for t in range(4 * NH):
                if t + 2 < 4 * NH:
                    prompt_scores(t + 2)
                pe.wait_ge(pa_norm, t + 1)
                if t == 0:
                    pe.wait_ge(vt_out, 10)
                if t >= 2:
                    pe.wait_ge(pa_copied, t - 1)
                for kj in range(t % 4 + 1):
                    mm = pe.transpose(ps_b[:, t % 2, kj * P:(kj + 1) * P], prob[:, t % 2, kj * P:(kj + 1) * P], ident)
                mm.then_inc(pa_trans, 1)
                if t % 4 == 0 and t:
                    prompt_values(t // 4 - 1)
            prompt_values(NH - 1)
            pe.wait_ge(dve_s, 3)
            for b in range(DB):
                mm = pe.transpose(ps_a[0:HC, 0, b * HC:(b + 1) * HC], p_new[:, b], ident[0:HC, 0:HC])
            mm.then_inc(pe_s, 1)
            pe.wait_ge(new_out, 2)
            pe.wait_ge(pt_out, DB)
            pe.wait_ge(pa_stored, NH)

            with pe.Fori(0, 2) as i:
                def values(s, u):
                    o = (ps_a, ps_b)[s % 2]
                    for slot in range(RING):
                        pg = 4 * u + slot
                        pe.wait_ge(page_loaded[slot], (16 * i + 4 * s + 33 + u) * 16)
                        if pg == 0:
                            pe.wait_ge(p_ready, 4 * i + s + 1)
                            pe.wait_ge(pv_out, 4 * i + s + 1)
                        c = ((pg % 4) * 4 + pg // 4) * HC
                        for n in range(2):
                            mm = pe.matmul(o[0:HC, n, :], p_seq[:, s % 2, c:c + HC],
                                           pages[:, slot, n * 512:(n + 1) * 512], start=pg == 0, stop=pg == PAGES - 1)
                        mm.then_inc(page_used, 1)
                for half_turn in range(2):
                    group(2 * i + 12 + half_turn, 4 * i + 24 + 2 * half_turn, 8, act_hi, act_lo,
                          after=lambda u, s=2 * half_turn: values(s + u // 4, u % 4))
            pe.wait_ge(pv_out, DB + 2)
            for a in range(2):
                for h in range(NH):
                    pe.matmul(ps_a[:, 0, h * HC + a * 16:h * HC + (a + 1) * 16], o_all[:, a, h * P:(h + 1) * P],
                              ident.rearrange("p (b n) -> p b n", b=4)[:, :, h * DL:(h + 1) * DL],
                              start=a == 0 and h == 0, stop=False, skip_group_check=True)
            for b in range(DB):
                mm = pe.matmul(ps_a[:, 0, 0:DB * HC].rearrange("p (h n) -> p h n", h=NH)[:, :, b * DL:(b + 1) * DL],
                               v_new[:, b], p_newT[:, b], start=False, stop=True, skip_group_check=True)
            mm.then_inc(new_done, 1)

            def pool_product(j):
                pe.wait_ge(d_ready, j + 1)
                f = 2 * (j % 2)
                group(G_POOL + j, Q_POOL, 1, f_hi[:, f:f + 2], f_lo[:, f:f + 2], k0=K_POOL[j])

            def ready2(u):
                return act_ready, KT + 2 * u + 2

            pool_product(0)
            pool_product(1)
            group(G_OUT, Q_POOL, 8, act_hi, act_lo, ready2, first=True, odd=1, units=range(0, 4))
            pool_product(2)
            pool_product(3)
            group(G_OUT, Q_POOL, 8, act_hi, act_lo, ready2, first=True, odd=1, units=range(4, 8))
            with pe.Fori(1, 8) as g:
                group(g + G_OUT, 2 * g + Q_OUT, 8, act_hi, act_lo)
            sum_squares(2 * KT)

            def ready3(u):
                return act_ready, 2 * KT + 2 * u + 2

            def gate_up(G, q, odd, ready=None, prev=2):
                for u in range(8):
                    ff_unit(G, q, u, u, 8, act_hi, act_lo, odd, ready, prev)

            def chunk(c, first=False):
                q0 = c * Q_CH + Q_FF
                g0 = c * G_CH + G_FF
                if first:
                    gate_up(g0, q0, 0, lambda kt: (act_ready, 2 * KT + kt + 1), prev=1)
                    sum_squares(3 * KT)
                    pe.wait_ge(var_ready, 3)
                    gate_up(g0 + 1, q0 + 2, 1)
                with pe.Fori(1 if first else 0, CH // 2) as j:
                    for odd in range(2):
                        gate_up(2 * j + g0 + odd, 4 * j + q0 + 2 * odd, odd)

                def f_ready(kt):
                    return f_split, c * CH + kt + 1
                with pe.Fori(0, 4) as d:
                    for k in range(4):
                        ff_unit(2 * d + g0 + CH + k % 2, d + q0 + 2 * CH, k, k // 2, 2, f_hi, f_lo, k % 2,
                                f_ready if k % 2 == 0 else None)

            chunk(0, first=True)
            with pe.Fori(1, NCH) as c:
                chunk(c)
            sum_squares(4 * KT)

        @block.vector
        def _(dve):
            def tile_of(t, m):
                return t[:, m] if isinstance(m, int) else t[:, bass.ds(m, 1)].rearrange("p a n -> p (a n)")

            def mean_square(n):
                dve.wait_ge(ss_done, n)
                dve.tensor_scalar(two(tmp), ps_a[:, :, 0:HN], 1.0 / D, EPS, ALU.mult, ALU.add).then_inc(var_ready, 1)

            def root_mean(n):
                dve.wait_ge(root_done, n)
                dve.reciprocal(rstd[:, :], rstd[:, :])
                dve.drain()
                dve.tensor_tensor(sq[:, 0], rstd[:, :], rstd[:, :], ALU.mult)
                dve.drain()
                dve.scalar_tensor_tensor(sq[:, 0], sq[:, 0], -0.5, tmp, ALU.mult, ALU.mult)
                dve.drain()
                dve.scalar_tensor_tensor(rstd[:, :], sq[:, 0], 1.5, rstd[:, :], ALU.add, ALU.mult)
                dve.drain().then_inc(rstd_ready, 1)

            def prep(kt, src, g, n0):
                dve.wait_ge(act_hi_done, n0 + kt + 1)
                dve.scalar_tensor_tensor(act_lo[:, kt], src[:, kt], g[:, kt:kt + 1], act_hi[:, kt].bitcast(F32),
                                         ALU.mult, ALU.subtract).then_inc(act_ready, 1)

            split_lo(dve, 0, 0)
            for kt in range(2):
                prep(kt, x_in, g_pre, 0)
            split_lo(dve, 0, 1)
            split_lo(dve, 0, 2)
            for u in range(8):
                split_lo(dve, 0, u + LEAD)
                for kt in (2 * u + 2, 2 * u + 3):
                    if kt < KT:
                        prep(kt, x_in, g_pre, 0)
            mean_square(1)
            split_lo(dve, 2, LEAD)
            root_mean(1)
            split_lo(dve, 2, 1 + LEAD)

            def to_stage(g, mt, odd):
                tile_done(dve, g, mt, 2 * g, 7)
                dve.tensor_tensor(two(stage[:, mt]), bank(mt, odd), two(rstd[:, :]), ALU.mult).then_inc(acc_free, 1)

            def rope(mt):
                x = stage[0:32, mt]
                dve.drain()
                dve.stream_shuffle(swap, x, [(i + 16) % 32 for i in range(32)])
                dve.drain()
                dve.tensor_tensor(x, x, cos_t, ALU.mult)
                dve.tensor_tensor(swap, swap, sin_t, ALU.mult)
                dve.drain()
                dve.tensor_tensor(x, x, swap, ALU.add).then_inc(st_ready, 1)

            def heads(g, odd=0):
                for mt in range(2):
                    to_stage(g, mt, odd)
                for mt in range(2):
                    rope(mt)

            dve.wait_ge(const_in, 48)
            heads(0)
            for u in range(2, 8):
                split_lo(dve, 2, u + LEAD)
            dve.wait_ge(st_copied, 2)
            heads(1, odd=1)
            with dve.Fori(2, 4) as g:
                for u in range(8):
                    split_lo(dve, 2 * g, u + LEAD)
                dve.wait_ge(st_copied, 2 * g)
                heads(g)

            def block_stats(b, quad):
                dve.wait_ge(scores_out, 4 * b + quad + 3)
                src = s_all[quad * HC:(quad + 1) * HC, bass.ds(b, 1)].rearrange("p a (k n) -> p (a k) n", k=2)
                for dst, op in ((gate, ALU.add), (bmax, ALU.max)):
                    dve.tensor_reduce(dst[:, bass.ds(b, 1), 2 * quad:2 * quad + 2].rearrange("p a k -> p (a k)"), src,
                                      AX.X, op)

            def kv_splits(g):
                for u in range(8):
                    split_lo(dve, 2 * g, u + LEAD)
                    if u in (3, 5, 7):
                        block_stats(g - 4, u // 2 - 1)

            with dve.Fori(4, 8) as g:
                kv_splits(g)
                dve.wait_ge(st_copied, 2 * g)
                dve.wait_ge(st_free, 2 * g - 6)
                heads(g)
                block_stats(g - 4, 3)
            with dve.Fori(8, 12) as g:
                kv_splits(g)
                dve.wait_ge(st_copied, 2 * g)
                dve.wait_ge(st_free, 2 * g - 6)
                for mt in range(2):
                    tile_done(dve, g, mt, 2 * g, 7)
                    dve.tensor_tensor(two(stage[:, mt]), bank(mt), two(rstd[:, :]), ALU.mult).then_inc(acc_free, 1)
                    dve.drain().then_inc(st_ready, 1)
                block_stats(g - 4, 3)

            dve.wait_ge(pe_s, 1)
            dve.tensor_tensor(p_new[:, :, :], ps[0:HC, 0, 0, 0:DB * HC].rearrange("p (b n) -> p b n", b=DB),
                              new_mask.unsqueeze(1).to_broadcast([HC, DB, HC]), ALU.add).then_inc(dve_s, 1)
            dve.drain()
            gj = gate[:, :, :].unsqueeze(2).to_broadcast([HC, DB, NBLK, NBLK])
            gi = gate[:, :, :].unsqueeze(3).to_broadcast([HC, DB, NBLK, NBLK])
            above = shared[0:HC, 0, 0:512].rearrange("p (b i j) -> p b i j", b=DB, i=NBLK)
            tied = shared[0:HC, 1, 0:512].rearrange("p (b i j) -> p b i j", b=DB, i=NBLK)
            dve.tensor_tensor(above, gj, gi, ALU.is_gt)
            dve.tensor_tensor(tied, gj, gi, ALU.is_equal)
            dve.drain()
            dve.tensor_tensor(tied, tied, below.unsqueeze(1).to_broadcast([HC, DB, NBLK, NBLK]), ALU.mult)
            dve.tensor_reduce(mx[:, 0], p_new[:, :, :], AX.X, ALU.max)
            dve.drain()
            dve.tensor_tensor(above, above, tied, ALU.add)
            dve.drain()
            dve.tensor_reduce(rank[:, :, :], above, AX.X, ALU.add)
            dve.drain()
            dve.tensor_scalar(rank[:, :, :], rank[:, :, :], float(TOPK), NEG, ALU.is_ge, ALU.mult)
            dve.drain()
            dve.tensor_tensor(bmax[:, :, :], bmax[:, :, :], rank[:, :, :], ALU.add)
            dve.drain()
            dve.tensor_reduce(mx[:, 1], bmax[:, :, :], AX.X, ALU.max)
            dve.drain()
            dve.tensor_tensor(mx[:, 2], mx[:, 0], mx[:, 1], ALU.max)
            dve.drain()
            dve.tensor_scalar(mx[:, 3], mx[:, 2], -SCALE, None, ALU.mult)
            dve.drain()
            dve.tensor_tensor(rank[:, :, :], rank[:, :, :], mx[:, 3].unsqueeze(2).to_broadcast([HC, DB, NBLK]), ALU.add)
            dve.drain()
            for quad in range(4):
                o = dve.tensor_copy(bias4[quad * HC:(quad + 1) * HC], rank[:, :, 2 * quad:2 * quad + 2])
            o.then_inc(dve_s, 1)

            def row_max(t):
                n = (t % 4 + 1) * P
                dve.wait_ge(pa_scores, t + 1)
                dve.tensor_reduce(col[:, 10 + t % 2:11 + t % 2], ps_a[:, t % 2, 0:n], AX.X, ALU.max)
                dve.drain()
                dve.tensor_scalar(col[:, t % 2:t % 2 + 1], col[:, 10 + t % 2:11 + t % 2], -SCALE, None, ALU.mult).then_inc(pa_max, 1)

            def decode_back(b):
                dve.wait_ge(pt_done, b + 1)
                dve.tensor_copy(s_all[:, b], ps[:, 1, b % 2, :]).then_inc(pt_out, 1)

            row_max(0)
            row_max(1)
            for t in range(4 * NH):
                n = (t % 4 + 1) * P
                dve.wait_ge(pa_exp, t + 1)
                dve.reciprocal(col[:, 12 + t % 2:13 + t % 2], col[:, 2 + t % 2:3 + t % 2])
                dve.drain()
                dve.tensor_scalar(prob[:, t % 2, 0:n], prob[:, t % 2, 0:n], col[:, 12 + t % 2:13 + t % 2], None,
                                  ALU.mult).then_inc(pa_norm, 1)
                if t + 2 < 4 * NH:
                    row_max(t + 2)
                if t % 4 == 3 and t > 4:
                    decode_back(t // 4 - 1)
            dve.wait_ge(act_s, DB)
            for quad in range(4):
                dve.tensor_copy(tot[:, :, 2 * quad:2 * quad + 2], esum[quad * HC:(quad + 1) * HC])
            dve.drain()
            dve.tensor_reduce(rinv[:, :], tot[:, :, :], AX.X, ALU.add)
            dve.drain()
            dve.reciprocal(rinv[:, :], rinv[:, :])
            dve.drain()
            dve.tensor_tensor(p_new[:, :, :], p_new[:, :, :], rinv[:, :].unsqueeze(2).to_broadcast([HC, DB, HC]),
                              ALU.mult).then_inc(dve_s, 1)
            decode_back(NH - 1)

            def ext_s(row):
                return row[:, HIST + SEQ:EXT].rearrange("p (b n) -> p b n", b=DB)[:, :, HIST:SEG]

            def samples(ap):
                return ap[:, SEQ:NT].rearrange("p (b l) -> p b l", b=DB)

            def ext_row(t, mt, g):
                tile_done(dve, g, mt, 2 * g, 7)
                row = ext[:, t]
                dve.tensor_tensor(row[:, HIST:HIST + HN], ps[:, mt, 0, 0:HN], rstd[:, 0:HN], ALU.mult)
                dve.tensor_tensor(row[:, HIST + HN:HIST + SEQ], ps[:, mt, 1, 0:SEQ - HN], rstd[:, HN:SEQ], ALU.mult)
                dve.tensor_tensor(ext_s(row), ps[:, mt, 1, SEQ - HN:HN].rearrange("p (b l) -> p b l", b=DB),
                                  samples(rstd), ALU.mult).then_inc(acc_free, 1)
                dve.drain().then_inc(ext_ready, 1)

            def pool(j):
                w = WINDOWS[j]
                dve.wait_ge(hist_placed, 1)
                rows, src, s, step = ext[:, 2 * j:2 * j + 2], None, 0, 1
                src = rows
                while step < w:
                    lo = 2 * step - 1
                    dst = win[:, s]
                    dve.tensor_tensor(dst[:, :, lo:EXT], src[:, :, lo:EXT], src[:, :, lo - step:EXT - step], ALU.add)
                    dve.drain()
                    src, s, step = dst, 1 - s, 2 * step
                dve.tensor_tensor(src[:, :, HIST:HIST + 16], src[:, :, HIST:HIST + 16],
                                  corr[:, j:j + 1, :].to_broadcast([P, 2, 16]), ALU.mult)
                dve.drain()
                dve.wait_ge(ext_stored, 32 * (j + 1))
                dve.scalar_tensor_tensor(rows[:, :, HIST:EXT], src[:, :, HIST:EXT], 1.0 / w, rows[:, :, HIST:EXT],
                                         ALU.mult, ALU.subtract).then_inc(pooled, 1)

            for j in range(4):
                g = 12 + j
                for u in range(8):
                    split_lo(dve, 2 * g, u + LEAD)
                    if u == 3 and j:
                        pool(j - 1)
                if j == 3:
                    dve.wait_ge(unit_used, 4 * 2 * g + NH // 2)
                    for h in range(NH):
                        dve.tensor_copy(act_hi[:, h, 0:SEQ], qT[:, h, 0:SEQ])
                    for h in range(NH):
                        if h == 0:
                            dve.drain()
                        dve.tensor_tensor(act_lo[:, h, 0:SEQ], qT[:, h, 0:SEQ], act_hi[:, h, 0:SEQ].bitcast(F32),
                                          ALU.subtract)
                for mt in range(2):
                    ext_row(2 * j + mt, mt, g)
            def window_lo(j):
                dve.wait_ge(d_hi, j + 1)
                if j == 1:
                    dve.wait_ge(new_done, 1)
                f = 2 * (j % 2)
                rows = ext[:, 2 * j:2 * j + 2]
                dve.tensor_tensor(f_lo[:, f:f + 2, 0:SEQ], rows[:, :, HIST:HIST + SEQ],
                                  f_hi[:, f:f + 2, 0:SEQ].bitcast(F32), ALU.subtract)
                for t in range(2):
                    i = dve.tensor_tensor(samples(f_lo[:, f + t]), ext_s(rows[:, t]),
                                          samples(f_hi[:, f + t]).bitcast(F32), ALU.subtract)
                i.then_inc(d_ready, 1)

            def pooled_lo(j):
                for mt in range(2):
                    t = NH + 2 * j + mt
                    dve.wait_ge(act_hi_done, KT + t + 1)
                    i = dve.scalar_tensor_tensor(two(act_lo[:, t]), bank(mt), pscale[:, 2 * j + mt:2 * j + mt + 1],
                                                 two(act_hi[:, t]).bitcast(F32), ALU.mult, ALU.subtract)
                    i.then_inc(act_ready, 1)
                    dve.drain().then_inc(acc_free, 1)

            window_lo(0)
            dve.wait_ge(act_hi_done, KT + NH)
            dve.tensor_tensor(act_lo[:, 0:NH, SEQ:NT], ps_a[:, 0, 0:DB * HC].rearrange("p (h n) -> p h n", h=NH),
                              act_hi[:, 0:NH, SEQ:NT].bitcast(F32), ALU.subtract).then_inc(act_ready, NH)
            window_lo(1)
            for k in range(12):
                split_lo(dve, Q_POOL, k + LEAD)
                if k in K_POOL:
                    pooled_lo(K_POOL.index(k))
                if k == 1:
                    pool(3)
                if k in (2, 3):
                    window_lo(k)

            dve.memset(sq_sum, 0.0)

            def mix_tiles(g, q, k, odd=0):
                for mt in range(2):
                    tile_done(dve, g + G_OUT, mt, q, k)
                    dve.tensor_copy(two(tile_of(acc, 2 * g + mt)), bank(mt, odd)).then_inc(acc_free, 1)
                    dve.drain().then_inc(mix_out, 1)
                for mt in range(2):
                    dve.drain()
                    dve.wait_ge(sq_done, 2 * g + KT + mt + 1)
                    dve.tensor_tensor(sq_sum, sq_sum, sq[:, mt], ALU.add).then_inc(sq_added, 1)

            mix_tiles(0, Q_POOL, K_OUT[-1], odd=1)
            with dve.Fori(1, 8) as g:
                for u in range(8):
                    split_lo(dve, 2 * g + Q_OUT, u + LEAD)
                mix_tiles(g, 2 * g + Q_OUT, 7)
            mean_square(2)
            root_mean(2)

            def resid(kt):
                if kt == 0:
                    dve.wait_ge(x_again, 64)
                if kt % 2 == 0:
                    dve.wait_ge(scaled, kt // 2 + 1)
                    dve.scalar_tensor_tensor(x2[:, kt], acc[:, kt], g_post[:, kt:kt + 1], x2[:, kt],
                                             ALU.mult, ALU.add).then_inc(x2_ready, 1)
                    return
                dve.scalar_tensor_tensor(acc[:, kt], acc[:, kt], g_post[:, kt:kt + 1], rstd[:, :], ALU.mult, ALU.mult)
                dve.drain()
                dve.tensor_tensor(x2[:, kt], acc[:, kt], x2[:, kt], ALU.add).then_inc(x2_ready, 1)

            def prep2(kt):
                if kt + 1 < KT:
                    resid(kt + 1)
                prep(kt, x2, g_fpre, 2 * KT)

            resid(0)
            prep2(0)
            prep2(1)

            def gate_group(c, j, odd, prepare=False):
                q, g, F = 2 * j + c * Q_CH + Q_FF + 2 * odd, j + c * G_CH + G_FF + odd, c * CH + j + odd
                pg, pu = banks(0, odd), banks(1, odd)
                for u in range(8):
                    split_lo(dve, q, u + LEAD)
                    if prepare and u < 7:
                        prep2(2 * u + 2)
                        prep2(2 * u + 3)
                if prepare:
                    mean_square(3)
                    root_mean(3)

                def p_(i):
                    return tile_of(par, F)[:, i:i + 1]
                dve.wait_ge(g_hist, F + 1)
                tile_done(dve, g, 0, q, 7)
                dve.tensor_tensor(g_ext[:, 2:2 + HN], pg[:, 0, 0:HN], rstd[:, 0:HN], ALU.mult)
                dve.tensor_tensor(g_ext[:, 2 + HN:2 + SEQ], pg[:, 1, 0:SEQ - HN], rstd[:, HN:SEQ], ALU.mult)
                dve.tensor_tensor(g_ext[:, 2 + SEQ:CEXT].rearrange("p (b n) -> p b n", b=DB)[:, :, 2:CSEG],
                                  pg[:, 1, SEQ - HN:HN].rearrange("p (b l) -> p b l", b=DB), samples(rstd),
                                  ALU.mult).then_inc(acc_free, 1)
                dve.drain().then_inc(g_ready, 1)
                tile_done(dve, g, 1, q, 7)
                dve.tensor_tensor(two(f_buf), pu[:, :, 0:HN], two(rstd[:, :]), ALU.mult).then_inc(acc_free, 1)
                dve.wait_ge(c_started, F + 1)
                dve.scalar_tensor_tensor(conv[:, 2:CEXT], g_ext[:, 1:CEXT - 1], p_(1), conv[:, 2:CEXT],
                                         ALU.mult, ALU.add)
                dve.drain()
                dve.scalar_tensor_tensor(conv[:, 2:CEXT], g_ext[:, 0:CEXT - 2], p_(0), conv[:, 2:CEXT],
                                         ALU.mult, ALU.add).then_inc(c_ready, 1)
                dve.wait_ge(gelu_done, F + 1)
                dve.tensor_tensor(f_buf[:, 0:SEQ], f_buf[:, 0:SEQ], conv[:, 2:2 + SEQ], ALU.mult)
                dve.tensor_tensor(samples(f_buf), samples(f_buf),
                                  conv[:, 2 + SEQ:CEXT].rearrange("p (b n) -> p b n", b=DB)[:, :, 2:CSEG],
                                  ALU.mult).then_inc(f_ready, 1)
                dve.wait_ge(f_hi_done, F + 1)
                dve.tensor_tensor(tile_of(f_lo, j + odd), f_buf, tile_of(f_hi, j + odd).bitcast(F32), ALU.subtract)\
                    .then_inc(f_split, 1)

            def chunk(c, first=False, last=False):
                q0, g0 = c * Q_CH + Q_FF, c * G_CH + G_FF
                if first:
                    gate_group(c, 0, 0, prepare=True)
                    gate_group(c, 0, 1)
                with dve.Fori(1 if first else 0, CH // 2) as j:
                    for odd in range(2):
                        gate_group(c, 2 * j, odd)

                def down(d, ahead):
                    for k in range(4):
                        if k < ahead:
                            split_lo(dve, d + q0 + 2 * CH, k + LEAD)
                        if k >= 2:
                            for mt in range(2):
                                i, g = k - 2, 2 * d + g0 + CH + k - 2
                                t = tile_of(acc, 4 * d + 2 * i + mt)
                                tile_done(dve, g, mt, d + q0 + 2 * CH, k)
                                if first:
                                    o = dve.tensor_copy(two(t), bank(mt, i))
                                else:
                                    o = dve.tensor_tensor(two(t), two(t), bank(mt, i), ALU.add)
                                o.then_inc(acc_free, 1)
                                if last:
                                    dve.drain().then_inc(mix_out, 1)
                    if last:
                        for i in range(4):
                            m = 4 * d + i
                            dve.drain()
                            dve.wait_ge(sq_done, m + 3 * KT + 1)
                            dve.tensor_tensor(sq_sum, sq_sum, sq[:, i % 2], ALU.add).then_inc(sq_added, 1)
                if last:
                    dve.memset(sq_sum, 0.0)
                with dve.Fori(0, 3 if last else 4) as d:
                    down(d, 4)
                if last:
                    down(3, 1)

            chunk(0, first=True)
            with dve.Fori(1, NCH - 1) as c:
                chunk(c)
            chunk(NCH - 1, last=True)
            mean_square(4)
            root_mean(4)
            for kt in range(KT):
                dve.scalar_tensor_tensor(acc[:, kt], acc[:, kt], g_fpost[:, kt:kt + 1], rstd[:, :],
                                         ALU.mult, ALU.mult).then_inc(scaled, 1)
                if kt not in Y_POOL:
                    dve.drain()
                    dve.tensor_tensor(x2[:, kt], acc[:, kt], x2[:, kt], ALU.add).then_inc(y_ready, 1)

        @block.gpsimd
        def _(pool):
            def tile_of(t, m):
                return t[:, m] if isinstance(m, int) else t[:, bass.ds(m, 1)].rearrange("p a n -> p (a n)")

            def row(t, i):
                return t[i] if isinstance(i, int) else t[bass.ds(i, 1)].rearrange("a p n -> p (a n)")

            def add_square(n0, kt):
                pool.wait_ge(sq_done, n0 + kt + 1)
                if kt == 0:
                    pool.tensor_copy(sq_sum, sq[:, 0]).then_inc(sq_added, 1)
                else:
                    pool.drain()
                    pool.tensor_tensor(sq_sum, sq_sum, sq[:, kt % 2], ALU.add).then_inc(sq_added, 1)

            pool.memset(q_blk[:, :], 0.0).then_inc(q_zeroed, 1)
            for kt in range(KT):
                add_square(0, kt)
            with pool.Fori(4, 8) as g:
                for mt in range(2):
                    pool.wait_ge(st_ready, 2 * g + mt + 1)
                    pool.dma_start(row(kT_out, 2 * g - 8 + mt), stage[:, mt]).then_inc(st_stored[mt], 16)
                for mt in range(2):
                    pool.wait_ge(st_stored[mt], (g - 3) * 16)
                pool.sem_inc(st_free, 2)
            with pool.Fori(8, 12) as g:
                for mt in range(2):
                    pool.wait_ge(st_ready, 2 * g + mt + 1)
                    pool.dma_start(row(vT_out, 2 * g - 16 + mt), stage[:, mt]).then_inc(st_stored[mt], 16)
                for mt in range(2):
                    pool.wait_ge(st_stored[mt], (g - 3) * 16)
                pool.sem_inc(st_free, 2)
            pool.wait_ge(pa_stored, NH)
            pool.memset(ext[:, :, 0:HIST], 0.0)
            pool.dma_start(hist_in, pool_hist).then_inc(hist_loaded, 16)
            pool.wait_ge(hist_loaded, 16)
            h4 = hist_in.rearrange("p (t b n) -> p t b n", t=NH, b=DB)
            for t in range(NH):
                pool.tensor_copy(ext[:, t, HIST + SEQ:EXT].rearrange("p (b n) -> p b n", b=DB)[:, :, 0:HIST], h4[:, t])
            pool.drain().then_inc(hist_placed, 1)
            for t in range(NH):
                pool.wait_ge(ext_ready, t + 1)
                pool.dma_start(ext_out[t], ext[:, t]).then_inc(ext_stored, 16)

            pool.wait_ge(rstd_ready, 2)
            for kt in range(KT):
                if kt % 2 == 0:
                    pool.tensor_tensor(acc[:, kt], acc[:, kt], rstd[:, :], ALU.mult).then_inc(scaled, 1)
                if kt >= 2:
                    add_square(2 * KT, kt - 2)
            add_square(2 * KT, KT - 2)
            add_square(2 * KT, KT - 1)
            pool.wait_ge(par_loaded, 16)
            pool.wait_ge(rstd_ready, 3)

            def conv_rows(F):
                seg = g_ext[:, 2 + SEQ:CEXT].rearrange("p (b n) -> p b n", b=DB)
                pool.tensor_copy(seg[:, :, 0:2], tile_of(par, F)[:, 4:NPAR].rearrange("p (b n) -> p b n", b=DB))\
                    .then_inc(g_hist, 1)
                pool.wait_ge(g_ready, F + 1)
                t = tile_of(tails, F)
                pool.tensor_copy(t[:, 0:2], g_ext[:, SEQ:SEQ + 2])
                pool.tensor_copy(t[:, 2:TAIL].rearrange("p (b n) -> p b n", b=DB), seg[:, :, DL:CSEG])
                pool.drain()
                pool.wait_ge(c_ready, F + 1)

            with pool.Fori(0, FT) as F:
                pool.memset(g_ext[:, 0:2], 0.0)
                conv_rows(F)
            pool.drain().then_inc(tails_out, 1)
            pool.dma_start(tail_out, tails).then_inc(out_done, 16)
            for kt in Y_POOL:
                pool.wait_ge(scaled, KT // 2 + kt + 1)
                pool.tensor_tensor(x2[:, kt], acc[:, kt], x2[:, kt], ALU.add).then_inc(y_pool, 1)
            pool.wait_ge(out_done, 16)
            pool.wait_ge(ext_stored, 16 * NH)
            for mt in range(2):
                pool.wait_ge(st_stored[mt], 16 * 8)


def _layout(a):
    import numpy as np

    def cols(w, nk, width=256):
        k, n = w.shape
        return w.reshape(k // 256, 2, P, n // width, width).transpose(3, 0, 2, 1, 4)

    def vec(v):
        return v.reshape(-1, P).T

    xT = np.concatenate([a["x_prompt"].reshape(SEQ, D), a["x_sample"].reshape(NS, D)]).T
    xT = np.ascontiguousarray(xT.reshape(KT, P, NT).transpose(1, 0, 2))
    w_in, half = a["w_in"][0], D // 2
    order = [3, 2, 1, 0]
    u = w_in[:, 0:half].reshape(D, 4, 256)[:, order].reshape(D, half)
    w_in = np.concatenate([w_in[:, half:], u], axis=1)
    w_out = a["w_out"][0]
    w_out = np.concatenate([w_out[half:], w_out[0:half].reshape(4, 256, D)[order].reshape(half, D)])
    wp = a["w_pool"][0][order]
    pool_out = np.concatenate([cols(wp[j], 0).reshape(-1, P, 512) for j in range(4)]
                              + [cols(w_out, 0).reshape(-1, P, 512)])
    first = np.empty(12, int)
    first[list(K_POOL)], first[list(K_OUT)] = range(4), range(4, 12)
    parts = [cols(w_in, 0).reshape(-1, P, 512), pool_out[first], pool_out[12:]]
    gate_up = np.stack([a["w_gate"][0].reshape(D, FT, P), a["w_up"][0].reshape(D, FT, P)], 2).reshape(D, FT * 256)
    gu = cols(gate_up, 0).reshape(NCH, CH * 8, P, 512)
    dn = a["w_down"][0].reshape(NCH, CH * P, D)
    dn = np.stack([cols(dn[c], 0).reshape(4, 2, 2, P, 512).transpose(0, 2, 1, 3, 4).reshape(16, P, 512)
                   for c in range(NCH)])
    parts.append(np.concatenate([gu, dn], axis=1).reshape(-1, P, 512))
    units = np.concatenate(parts)
    assert units.shape[0] == UNITS
    kc = np.ascontiguousarray(a["cache_k"][0].transpose(0, 3, 1, 2)).reshape(N_PHYS, P, NH * PAGE)
    vc = np.ascontiguousarray(a["cache_v"][0].transpose(0, 2, 1, 3)).reshape(N_PHYS, PAGE, NH * P)
    ps = a["pool_scale"][0].reshape(4, 256)[order].reshape(-1)
    gains = np.concatenate([vec(a[n][0]) for n in ("g_mix_pre", "g_mix_post", "g_ffn_pre", "g_ffn_post")]
                           + [vec(ps)], axis=1)
    ph = a["state_pool"][0].reshape(DB, HIST, 4, 256)[:, :, order].reshape(DB, HIST, NH, P)
    pool_hist = np.ascontiguousarray(ph.transpose(3, 2, 0, 1)).reshape(P, NH * DB * HIST)
    cw = a["conv_w"][0].reshape(3, FT, P).transpose(2, 1, 0)
    cb = a["conv_b"][0].reshape(FT, P).T[:, :, None]
    ch = a["state_conv"][0].reshape(DB, 2, FT, P).transpose(3, 2, 0, 1).reshape(P, FT, 2 * DB)
    conv_par = np.concatenate([cw, cb, ch], axis=2)
    pos = np.concatenate([np.arange(SEQ), np.tile(PAGES * PAGE + np.arange(DL), DB)]).astype(np.float32)
    inv = np.float32(500000.0) ** (-np.arange(16, dtype=np.float32) * np.float32(2.0 / 32))
    ang = (inv[:, None].astype(np.float32) * pos[None, :]).astype(np.float32)
    c, s = np.cos(ang).astype(np.float32), np.sin(ang).astype(np.float32)
    rope_tab = np.stack([np.concatenate([c, c]), np.concatenate([-s, s])], axis=1)
    cst = np.zeros((P, 544), np.float32)
    cst[:, 0:128] = np.eye(P)
    cst[:, 128:256] = 1.0
    i = np.arange(P)
    cst[:, 256:384] = np.where(i[None, :] <= i[:, None], 0.0, NEG)
    j = np.arange(HC)
    same = (j[:, None] // DL == j[None, :] // DL) & (j[None, :] % DL <= j[:, None] % DL)
    cst[0:NS, 384:416] = np.where(same, 0.0, NEG)
    b = np.arange(NBLK)
    cst[0:NS, 416:480] = (b[None, :] < b[:, None]).astype(np.float32).reshape(1, 64)
    t = np.arange(16)
    cst[:, 480:544] = np.concatenate([w / np.minimum(t + 1, w) for w in WINDOWS])[None, :]
    table = np.ascontiguousarray(a["page_table"]).reshape(DB * 2, PAGES // 2)
    return {"xT": xT, "units": units, "kcache": kc, "vcache": vc, "table": table, "gains": gains,
            "pool_hist": pool_hist, "conv_par": conv_par, "rope_tab": rope_tab, "consts": cst}


_OUTS = {"yT": (P, KT, NT), "kT_out": (NH, P, NT), "vT_out": (NH, P, NT), "ext_out": (NH, P, EXT),
         "tail_out": (P, FT, TAIL)}


def kernel(**inputs):
    import numpy as np
    import concourse.bacc as bacc
    from concourse.bass_utils import run_bass_kernel_spmd

    a = {k: np.asarray(v) for k, v in inputs.items()}
    arrays = {k: np.ascontiguousarray(v) for k, v in _layout(a).items()}
    nc = bacc.Bacc("TRN2", target_bir_lowering=False, num_devices=1)
    aps = {k: nc.dram_tensor(k, v.shape, mybir.dt.from_np(v.dtype), kind="ExternalInput").ap()
           for k, v in arrays.items()}
    aps |= {k: nc.dram_tensor(k, s, F32, kind="ExternalOutput").ap() for k, s in _OUTS.items()}
    build(nc, **aps)
    r = run_bass_kernel_spmd(nc, [arrays], core_ids=[0]).results[0]
    y = r["yT"].transpose(2, 1, 0).reshape(NT, D)

    def heads(t):
        t = t.transpose(0, 2, 1)
        dec = t[:, SEQ:].reshape(NH, DB, DL, P).transpose(1, 0, 2, 3)
        return t[None, None, :, 0:SEQ], dec[None]

    kp, ks = heads(r["kT_out"])
    vp, vs = heads(r["vT_out"])
    e = r["ext_out"].reshape(4, 2, P, EXT)[[3, 2, 1, 0]].reshape(NH * P, EXT)
    pp = e[:, SEQ:SEQ + HIST].T
    pd = e[:, HIST + SEQ:].reshape(NH * P, DB, SEG)[:, :, DL:].transpose(1, 2, 0)
    t = r["tail_out"].transpose(2, 1, 0).reshape(TAIL, FF)
    out = (y[0:SEQ][None], y[SEQ:].reshape(DB, DL, D), kp, vp, ks, vs, pp[None, None], pd[None],
           t[0:2][None, None], t[2:].reshape(1, DB, 2, FF))
    return tuple(np.ascontiguousarray(o) for o in out)
```
